# Optimizing a Trainium2 kernel written in Bass

```python
import math
import jax, jax.numpy as jnp
from jax import lax
import numpy as np

D_MODEL = 1024
BATCH = 1
SEQ = 256
DEPTH = 1

CHUNK = 64
D_MIX = D_MODEL
RET_WIDTH = D_MIX // 2
CONV_WIDTH = D_MIX - RET_WIDTH
RET_HEADS = 8
RET_HEAD_DIM = RET_WIDTH // RET_HEADS
CONV_GROUPS = 8
CONV_GROUP_DIM = CONV_WIDTH // CONV_GROUPS
CONV_K = 3
ROPE_BASE = 10000.0
N_GROUPS = 4
EXPERTS_PER_GROUP = 8
TOP_K = 2
D_EXPERT = D_MODEL // 2
EPS = 1e-6
GN_EPS = 1e-5
IN_COLS = 4 * RET_WIDTH + 3 * CONV_WIDTH

kernel_name = "hybrid_retention_shortconv_hmoe_adaln"

def rms_norm(x, g):
    xf = x.astype(jnp.float32)
    y = xf * lax.rsqrt(jnp.mean(xf * xf, axis=-1, keepdims=True) + EPS)
    return (y * g.astype(jnp.float32)).astype(x.dtype)

def rotary(positions, dim, dtype):
    inv_freq = ROPE_BASE ** (-jnp.arange(0, dim, 2, dtype=jnp.float32) / dim)
    ang = positions.astype(jnp.float32)[..., None] * inv_freq
    return jnp.cos(ang)[:, :, None, :].astype(dtype), jnp.sin(ang)[:, :, None, :].astype(dtype)

def apply_rotary(t, cos, sin):
    t1, t2 = jnp.split(t, 2, axis=-1)
    return jnp.concatenate([t1 * cos - t2 * sin, t2 * cos + t1 * sin], axis=-1)

def retention(q, k, v, positions):
    B, S, H, dh = q.shape
    nc = S // CHUNK
    dt = q.dtype
    cos, sin = rotary(positions, dh, dt)
    q = apply_rotary(q, cos, sin)
    k = apply_rotary(k, cos, sin) * (dh ** -0.5)

    def to_chunks(t):
        return t.reshape(B, nc, CHUNK, H, dh).transpose(0, 3, 1, 2, 4)

    qc, kc, vc = to_chunks(q), to_chunks(k), to_chunks(v)
    log_gamma = jnp.log1p(-jnp.exp2(-5.0 - jnp.arange(H, dtype=jnp.float32)))
    idx = jnp.arange(CHUNK, dtype=jnp.float32)
    dist = jnp.abs(idx[:, None] - idx[None, :])
    d_intra = jnp.exp(log_gamma[:, None, None] * dist).astype(dt)
    k_decay = jnp.exp(log_gamma[:, None] * (CHUNK - 1 - idx)).astype(dt)
    q_decay = jnp.exp(log_gamma[:, None] * (idx + 1.0)).astype(dt)
    chunk_decay = jnp.exp(log_gamma * CHUNK).astype(dt)

    scores = jnp.einsum('bhncd,bhnmd->bhncm', qc, kc) * d_intra[None, :, None]
    y_intra = jnp.einsum('bhncm,bhnmd->bhncd', scores, vc)

    kv = jnp.einsum('bhnmd,bhnme->bhnde', kc * k_decay[None, :, None, :, None], vc)

    def step(state, kv_i):
        return state * chunk_decay[None, :, None, None] + kv_i, state

    _, s_prev = lax.scan(step, jnp.zeros((B, H, dh, dh), kv.dtype), jnp.moveaxis(kv, 2, 0))
    s_prev = jnp.moveaxis(s_prev, 0, 2)
    y_inter = jnp.einsum('bhncd,bhnde->bhnce', qc * q_decay[None, :, None, :, None], s_prev)

    y = y_intra + y_inter
    return y.transpose(0, 2, 3, 1, 4).reshape(B, S, H, dh)

def group_norm_heads(y):
    yf = y.astype(jnp.float32)
    mu = jnp.mean(yf, axis=-1, keepdims=True)
    var = jnp.mean(jnp.square(yf - mu), axis=-1, keepdims=True)
    return ((yf - mu) * lax.rsqrt(var + GN_EPS)).astype(y.dtype)

def mixer(h, positions, w_in, conv_w, conv_b, beta_ret, beta_conv, w_out):
    B, S, _ = h.shape
    proj = h @ w_in
    q, k, v, g, b_gate, c_gate, h_conv = jnp.split(
        proj, np.cumsum([RET_WIDTH] * 4 + [CONV_WIDTH] * 2).tolist(), axis=-1)

    shp = (B, S, RET_HEADS, RET_HEAD_DIM)
    y_ret = retention(q.reshape(shp), k.reshape(shp), v.reshape(shp), positions)
    y_ret = group_norm_heads(y_ret).reshape(B, S, RET_WIDTH)
    y_ret = jax.nn.silu(g) * y_ret * beta_ret

    u = c_gate * h_conv
    conv = lax.conv_general_dilated(
        u, conv_w[:, None, :], window_strides=(1,), padding=[(CONV_K - 1, 0)],
        dimension_numbers=('NWC', 'WIO', 'NWC'), feature_group_count=CONV_WIDTH) + conv_b
    y_conv = (b_gate * conv).reshape(B, S, CONV_GROUPS, CONV_GROUP_DIM)
    y_conv = rms_norm(y_conv, jnp.ones((CONV_GROUP_DIM,), y_conv.dtype)).reshape(B, S, CONV_WIDTH)
    y_conv = y_conv * beta_conv

    return jnp.concatenate([y_ret, y_conv], axis=-1) @ w_out

def hier_moe(h, wg, bg, we, be, w_gate, w_up, w_down):
    B, S, D = h.shape
    t = h.reshape(-1, D)
    n = t.shape[0]
    g_prob = jax.nn.softmax((t @ wg + bg).astype(jnp.float32), axis=-1)
    g_top, g_idx = lax.top_k(g_prob, 1)
    e_logits = (t @ we + be).astype(jnp.float32).reshape(n, N_GROUPS, EXPERTS_PER_GROUP)
    e_sel = jnp.take_along_axis(e_logits, g_idx[:, :, None], axis=1)[:, 0]
    e_prob = jax.nn.softmax(e_sel, axis=-1)
    e_top, e_idx = lax.top_k(e_prob, TOP_K)
    e_w = e_top / jnp.sum(e_top, axis=-1, keepdims=True) * g_top
    within = jnp.sum(jax.nn.one_hot(e_idx, EXPERTS_PER_GROUP, dtype=jnp.float32) * e_w[..., None], axis=1)
    combine = (jax.nn.one_hot(g_idx[:, 0], N_GROUPS, dtype=jnp.float32)[:, :, None]
               * within[:, None, :]).astype(t.dtype)
    out = jnp.zeros_like(t)
    for gi in range(N_GROUPS):
        a = jnp.einsum('nd,edf->nef', t, w_gate[gi])
        u = jnp.einsum('nd,edf->nef', t, w_up[gi])
        hid = jax.nn.silu(a) * u * combine[:, gi, :, None]
        out = out + jnp.einsum('nef,efd->nd', hid, w_down[gi])
    return out.reshape(B, S, D)

def setup_inputs(seed: int = 0) -> dict:
    key = jax.random.key(seed)
    ks = jax.random.split(key, 24)
    f32 = jnp.float32
    nrm = lambda k, shape, s: jax.random.normal(k, shape, f32) * s
    x = jax.random.normal(ks[0], (BATCH, SEQ, D_MODEL), f32)
    c = jax.random.normal(ks[1], (BATCH, D_MODEL), f32)
    offset = jax.random.randint(ks[2], (BATCH, 1), 0, 4096, dtype=jnp.int32)
    positions = (offset + jnp.arange(SEQ, dtype=jnp.int32)[None, :]).astype(jnp.int32)
    ge = N_GROUPS * EXPERTS_PER_GROUP
    return {
        "x": x,
        "c": c,
        "positions": positions,
        "ada_w": nrm(ks[3], (DEPTH, D_MODEL, 6 * D_MODEL), 0.5 * D_MODEL ** -0.5),
        "ada_b": nrm(ks[4], (DEPTH, 6 * D_MODEL), 0.02),
        "norm_mix_g": 1.0 + nrm(ks[5], (DEPTH, D_MODEL), 0.02),
        "norm_ffn_g": 1.0 + nrm(ks[6], (DEPTH, D_MODEL), 0.02),
        "w_in": nrm(ks[7], (DEPTH, D_MODEL, IN_COLS), D_MODEL ** -0.5),
        "conv_w": nrm(ks[8], (DEPTH, CONV_K, CONV_WIDTH), CONV_K ** -0.5),
        "conv_b": nrm(ks[9], (DEPTH, CONV_WIDTH), 0.02),
        "beta_ret": 1.0 + nrm(ks[10], (DEPTH, RET_WIDTH), 0.02),
        "beta_conv": 1.0 + nrm(ks[11], (DEPTH, CONV_WIDTH), 0.02),
        "w_out": nrm(ks[12], (DEPTH, D_MIX, D_MODEL), D_MIX ** -0.5),
        "router_group_w": nrm(ks[13], (DEPTH, D_MODEL, N_GROUPS), D_MODEL ** -0.5),
        "router_group_b": nrm(ks[14], (DEPTH, N_GROUPS), 0.01),
        "router_expert_w": nrm(ks[15], (DEPTH, D_MODEL, ge), D_MODEL ** -0.5),
        "router_expert_b": nrm(ks[16], (DEPTH, ge), 0.01),
        "expert_w_gate": nrm(ks[17], (DEPTH, N_GROUPS, EXPERTS_PER_GROUP, D_MODEL, D_EXPERT), D_MODEL ** -0.5),
        "expert_w_up": nrm(ks[18], (DEPTH, N_GROUPS, EXPERTS_PER_GROUP, D_MODEL, D_EXPERT), D_MODEL ** -0.5),
        "expert_w_down": nrm(ks[19], (DEPTH, N_GROUPS, EXPERTS_PER_GROUP, D_EXPERT, D_MODEL), D_EXPERT ** -0.5),
        "norm_final_g": 1.0 + nrm(ks[20], (D_MODEL,), 0.02),
    }

def reference(x, c, positions, ada_w, ada_b, norm_mix_g, norm_ffn_g, w_in, conv_w, conv_b,
              beta_ret, beta_conv, w_out, router_group_w, router_group_b, router_expert_w,
              router_expert_b, expert_w_gate, expert_w_up, expert_w_down, norm_final_g):
    for l in range(DEPTH):
        mod = jax.nn.silu(c) @ ada_w[l] + ada_b[l]
        shift_m, scale_m, gate_m, shift_f, scale_f, gate_f = jnp.split(mod[:, None, :], 6, axis=-1)

        h = rms_norm(x, norm_mix_g[l]) * (1.0 + scale_m) + shift_m
        x = x + gate_m * mixer(h, positions, w_in[l], conv_w[l], conv_b[l],
                               beta_ret[l], beta_conv[l], w_out[l])

        h = rms_norm(x, norm_ffn_g[l]) * (1.0 + scale_f) + shift_f
        x = x + gate_f * hier_moe(h, router_group_w[l], router_group_b[l], router_expert_w[l],
                                  router_expert_b[l], expert_w_gate[l], expert_w_up[l],
                                  expert_w_down[l])
    return rms_norm(x, norm_final_g)


_drawn_inputs = setup_inputs


def setup_inputs(seed=0):
    import zlib

    import numpy as np

    out = dict(_drawn_inputs(seed))
    spreads = {}
    factors = {'norm_mix_g': 4.241,
     'norm_ffn_g': 4.859,
     'conv_b': 64.0,
     'beta_ret': 8.0,
     'beta_conv': 8.0,
     'router_group_b': 8.0,
     'router_expert_b': 8.0,
     'norm_final_g': 9.044}
    for name, (base, spread) in spreads.items():
        noise = np.random.default_rng([zlib.crc32(name.encode()), seed]).standard_normal(out[name].shape)
        drawn = base * np.exp(spread * noise) if base else spread * noise
        out[name] = __import__('jax').numpy.asarray(drawn.astype(out[name].dtype))
    for name, factor in factors.items():
        out[name] = (out[name] * factor).astype(out[name].dtype)
    return out
```

```python
from contextlib import ExitStack

import concourse.bass as bass
import numpy as np
from concourse import mybir

F32 = mybir.dt.float32
I32 = mybir.dt.int32
ALU = mybir.AluOpType
ACT = mybir.ActivationFunctionType
AX = mybir.AxisListType

P = 128
EPS = 1e-6
GN_EPS = 1e-5
ROPE_BASE = 10000.0
TWO_PI = 2.0 * np.pi
PI_BELOW = 3.1415925
TWO_PI_HI = 6.28125
TWO_PI_MID = float(np.float32(0.0019350051879882812))
TWO_PI_LO = float(np.float32(TWO_PI - TWO_PI_HI - TWO_PI_MID))
ROUND = 12582912.0
SLOTS = 64
RING = 6


def hybrid_retention_moe_layer(nc, x, c, positions, ada_w, ada_b, norm_mix_g, norm_ffn_g, w_in, conv_w, conv_b,
                               beta_ret, beta_conv, w_out, router_group_w, router_group_b, router_expert_w,
                               router_expert_b, expert_w_gate, expert_w_up, expert_w_down, norm_final_g, out):
    _, S, D = x.shape
    TT = S // P
    KD = D // P
    CHUNK = 64
    RW = D // 2
    H = 8
    DH = RW // H
    HALF = DH // 2
    CT4 = RW // P
    KC = conv_w.shape[1]
    G = router_group_w.shape[2]
    EG = expert_w_gate.shape[2]
    E = G * EG
    F = expert_w_gate.shape[4]
    KF = F // P
    PAIRS = E // 2
    U = 512
    MAX_PASS = S // SLOTS
    assert S == 256 and D == 1024 and RW == 512 and F == 512 and DH == CHUNK == 64

    gate_rows = expert_w_gate.rearrange("l g e (p j) f -> (l g e) p (j f)", p=P)
    up_rows = expert_w_up.rearrange("l g e (p j) f -> (l g e) p (j f)", p=P)
    down_rows = expert_w_down.rearrange("l g e (p j) f -> (l g e) p (j f)", p=P)
    ada_rows = ada_w.rearrange("l (p j) n -> (l p) j n", p=P)
    win_rows = w_in.rearrange("l (p j) n -> (l p) j n", p=P)
    wout_rows = w_out.rearrange("l (t p) n -> (l p) t n", p=P)

    units = [("ada", u) for u in range(4)]
    for k in range(7):
        units += [("win", k), ("ada", 4 + k)]
    units += [("ada", 11), ("wout", 0), ("wout", 1)]
    unit_index = {key: n for n, key in enumerate(units)}
    NU = len(units)

    with ExitStack() as ctx:
        def sb(name, shape, dt=F32):
            return ctx.enter_context(nc.sbuf_tensor(name, shape, dt))

        def sem(name):
            return ctx.enter_context(nc.semaphore(name))

        ring = [sb(f"ring{i}", [P, KD * U]) for i in range(RING)]
        expert_slot = [ring[(NU + k) % RING] for k in range(6)]
        gate_w = [expert_slot[k][:, :].rearrange("p (j f) -> p j f", j=KD) for k in (0, 1)]
        up_w = [expert_slot[k][:, :].rearrange("p (j f) -> p j f", j=KD) for k in (2, 3)]
        down_w = [expert_slot[k][:, :].rearrange("p (j d) -> p j d", j=KF) for k in (4, 5)]

        x_sb = sb("x_sb", [P, TT, D])
        xn = sb("xn", [P, TT, D])
        hT = sb("hT", [P, KD, S])
        yT = hT
        gate_mix = sb("gate_mix", [P, D])
        gate_ffn = sb("gate_ffn", [P, D])
        final_g = sb("final_g", [P, D])
        ident = sb("ident", [P, P])
        before = sb("before", [P, P])
        ones = sb("ones", [P, P])
        fold = sb("fold", [P, P])
        conv_groups = sb("conv_groups", [P, P])
        slot_ids = sb("slot_ids", [P, (MAX_PASS + 1) * SLOTS])
        rev = sb("rev", [P, EG])
        eps_col = sb("eps_col", [P, 2])
        router_w = sb("router_w", [P, KD, G + E])
        router_b = sb("router_b", [P, G + E])
        mod_bias = sb("mod_bias", [P, 6, KD])
        norm_g = sb("norm_g", [P, 2, KD])
        modcol = sb("modcol", [P, 4, KD])
        scale_a = sb("scale_a", [P, 2, KD])
        small_rows = sb("small_rows", [(KC + 3) * CT4, P])
        small_cols = sb("small_cols", [P, (KC + 3) * CT4])
        ssq = sb("ssq", [P, 4, TT])
        rms = sb("rms", [P, 4, TT])
        part = sb("part", [P, 2, U])
        posm = sb("posm", [P, TT, E])
        combine = sb("combine", [P, TT, E])
        npass_i = sb("npass_i", [1, 1], I32)

        arena = sb("arena", [P, 12736])
        taken = [0]

        def front(shape):
            n = int(np.prod(shape))
            ap = arena[:, taken[0]:taken[0] + n]
            taken[0] += n
            assert taken[0] <= 12736
            if len(shape) == 1:
                return ap
            names = "abcd"[:len(shape)]
            return ap.rearrange("p (%s) -> p %s" % (" ".join(names), " ".join(names)),
                                **{k: v for k, v in zip(names, shape)})

        cvec = front([4, KD])
        c_wide = front([KD, 32])
        trig = front([2, TT, HALF])
        trig_arg = front([4, 2, TT, HALF])
        inv_freq = front([HALF])
        pos_f = front([TT])
        dist = front([S])
        decay = front([H, S])
        q_rot = front([TT, RW])
        k_rot = front([TT, RW])
        v_sb = front([TT, RW])
        g_silu = front([TT, RW])
        tmp_c = front([RW])
        tmp_s = front([RW])
        weighted = front([2, S + P])
        kT = front([CT4, S])
        b_sb = front([CT4, S])
        qT = sb("qT", [P, CT4, S])
        u_pad = front([CT4, S + KC - 1])
        lg = front([TT, G + E])
        rt = front([16, TT, EG])
        within8 = front([2, TT, EG])
        msk = front([TT, E])
        ohe = front([TT, E])
        cnt = front([4])
        conv_y = sb("conv_y", [P, CT4, S])
        pos_i = sb("pos_i", [P, TT], I32)
        groups = sb("groups", [P, 3, TT * H])

        taken[0] = 2048
        xgT = front([KD, 2 * SLOTS])
        pick = front([TT, 2 * SLOTS])
        place = front([TT, 2 * SLOTS])
        placeT = front([TT * P])
        hid = front([F])
        ea = front([F])
        hidT = front([KF, 2 * SLOTS])
        y_sb = front([D])

        ps = ctx.enter_context(nc.psum_tensor("ps", [P, 8, 512], F32))

        def banks(a, n):
            return ps[:, a:a + n, :].rearrange("p b c -> p (b c)")

        ps_part = banks(0, 1)
        ps_fold = banks(1, 1)
        ps_p = banks(2, 2)
        ps_q = banks(4, 2)
        ps_s = banks(6, 2)
        ps_yT = banks(0, 2)
        ps_acc = banks(0, 4)
        ps_xy = banks(4, 2)
        ps_gate = banks(6, 1)
        ps_up = banks(7, 1)

        ring_full = [sem(f"ring_full{i}") for i in range(RING)]
        gate_full = [sem("gate_full0"), sem("gate_full1")]
        up_full = [sem("up_full0"), sem("up_full1")]
        down_full = [sem("down_full0"), sem("down_full1")]
        gate_done = sem("gate_done")
        up_done = sem("up_done")
        down_done = sem("down_done")
        x_in = sem("x_in")
        c_in = sem("c_in")
        pos_in = sem("pos_in")
        mod_in = sem("mod_in")
        rows_in = sem("rows_in")
        router_in = sem("router_in")
        wide_in = sem("wide_in")
        out_written = sem("out_written")
        consts = sem("consts")
        act_step = sem("act_step")
        dve_step = sem("dve_step")
        pool_step = sem("pool_step")
        c_exp = sem("c_exp")
        c_ready = sem("c_ready")
        squares = sem("squares")
        rms_ready = sem("rms_ready")
        root_ready = sem("root_ready")
        xn_ready = sem("xn_ready")
        trig_arg_ready = sem("trig_arg_ready")
        trig_ready = sem("trig_ready")
        decay_ready = sem("decay_ready")
        decay_masked = sem("decay_masked")
        xT_done = sem("xT_done")
        part_done = sem("part_done")
        part_read = sem("part_read")
        fold_done = sem("fold_done")
        fold_read = sem("fold_read")
        smallT_done = sem("smallT_done")
        smallT_read = sem("smallT_read")
        scales_ready = sem("scales_ready")
        hT_act = sem("hT_act")
        hT_dve = sem("hT_dve")
        win_done = sem("win_done")
        q_ready = sem("q_ready")
        k_ready = sem("k_ready")
        v_ready = sem("v_ready")
        g_exp = sem("g_exp")
        g_ready = sem("g_ready")
        b_ready = sem("b_ready")
        c_read = sem("c_read")
        u_ready = sem("u_ready")
        qT_done = sem("qT_done")
        qT_ready = sem("qT_ready")
        kT_done = sem("kT_done")
        kT_ready = sem("kT_ready")
        scores_done = sem("scores_done")
        weighted_ready = sem("weighted_ready")
        pv_done = sem("pv_done")
        convy_ready = sem("convy_ready")
        convsq_ready = sem("convsq_ready")
        convms_done = sem("convms_done")
        convroot_ready = sem("convroot_ready")
        yT_conv = sem("yT_conv")
        centered = sem("centered")
        centered_sq = sem("centered_sq")
        gnvar_ready = sem("gnvar_ready")
        gnroot_ready = sem("gnroot_ready")
        yret_ready = sem("yret_ready")
        yretT_done = sem("yretT_done")
        yT_ret = sem("yT_ret")
        wout_done = sem("wout_done")
        x1_ready = sem("x1_ready")
        logits_done = sem("logits_done")
        group_shift = sem("group_shift")
        group_exp = sem("group_exp")
        expert_shift = sem("expert_shift")
        expert_exp = sem("expert_exp")
        mask_ready = sem("mask_ready")
        rank_done = sem("rank_done")
        npass_ready = sem("npass_ready")
        route_ready = sem("route_ready")
        zero_ready = sem("zero_ready")
        pick_ready = sem("pick_ready")
        place_ready = sem("place_ready")
        gather_done = sem("gather_done")
        xg_lo = sem("xg_lo")
        xg_hi = sem("xg_hi")
        ea_ready = sem("ea_ready")
        hid_ready = sem("hid_ready")
        turned = sem("turned")
        hidT_ready = sem("hidT_ready")
        placeT_ready = sem("placeT_ready")
        y_lo = sem("y_lo")
        y_hi = sem("y_hi")
        acc_done = sem("acc_done")
        out_ready = sem("out_ready")

        block = ctx.enter_context(nc.Block())

        def expert_view(ap, e):
            return ap[bass.ds(e, 1)].rearrange("e p n -> p (e n)")

        def unit_used(n):
            kind, u = units[n]
            return {"ada": (part_done, u + 1), "win": (win_done, u + 1), "wout": (wout_done, TT)}[kind]

        @block.sync
        def _(sp):
            for n, (kind, u) in enumerate(units):
                if n >= RING:
                    sp.wait_ge(*unit_used(n - RING))
                src = {"ada": ada_rows, "win": win_rows, "wout": wout_rows}[kind]
                sp.dma_start(ring[n % RING][:, :].rearrange("p (j f) -> p j f", j=KD),
                             src[:, :, u * U:(u + 1) * U]).then_inc(ring_full[n % RING], 16)
            first = [(gate_rows, gate_full), (up_rows, up_full), (down_rows, down_full)]
            for k in range(6):
                rows, full = first[k // 2]
                sp.wait_ge(*unit_used(NU - RING + k))
                sp.dma_start(expert_slot[k][:, :], rows[k % 2]).then_inc(full[k % 2], 16)
            sp.wait_ge(npass_ready, 1)
            npass = sp.value_load(npass_i[0:1, 0:1], min_val=1, max_val=MAX_PASS)
            with sp.Fori(1, npass * PAIRS) as g:
                e = (g % PAIRS) * 2
                sp.wait_ge(gate_done, g)
                for k in range(2):
                    sp.dma_start(expert_slot[k][:, :], expert_view(gate_rows, e + k)).then_inc(gate_full[k], 16)
                sp.wait_ge(up_done, g)
                for k in range(2):
                    sp.dma_start(expert_slot[2 + k][:, :], expert_view(up_rows, e + k)).then_inc(up_full[k], 16)
                sp.wait_ge(down_done, g)
                for k in range(2):
                    sp.dma_start(expert_slot[4 + k][:, :], expert_view(down_rows, e + k)).then_inc(down_full[k], 16)

        @block.gpsimd
        def _(pool):
            steps = [0]

            def step(ins):
                ins.then_inc(pool_step, 1)
                steps[0] += 1
                pool.wait_ge(pool_step, steps[0])

            step(nc.gpsimd.memset(ones[:, :], 1.0))
            step(nc.gpsimd.memset(fold[:, :], 1.0 / 32))
            step(nc.gpsimd.memset(ident[:, :], 0.0))
            step(nc.gpsimd.affine_select(out=ident[:, :], in_=ident[:, :], compare_op=ALU.not_equal, fill=1.0, base=0,
                                    pattern=[[-1, P]], channel_multiplier=1))
            step(nc.gpsimd.memset(before[:, :], 1.0))
            step(nc.gpsimd.affine_select(out=before[:, :], in_=before[:, :], compare_op=ALU.is_gt, fill=0.0, base=0,
                                    pattern=[[1, P]], channel_multiplier=-1))
            for i in range(HALF):
                f = float(np.float32(ROPE_BASE ** (-2.0 * i / DH)))
                step(nc.gpsimd.memset(inv_freq[:, i:i + 1], f))
            step(nc.gpsimd.iota(dist, pattern=[[1, S]], base=0, channel_multiplier=-1,
                           allow_small_or_imprecise_dtypes=True))
            step(nc.gpsimd.iota(slot_ids[:, :], pattern=[[1, (MAX_PASS + 1) * SLOTS]], base=0, channel_multiplier=0,
                           allow_small_or_imprecise_dtypes=True))
            step(nc.gpsimd.iota(rev[:, :], pattern=[[-1, EG]], base=EG, channel_multiplier=0,
                           allow_small_or_imprecise_dtypes=True))
            step(nc.gpsimd.memset(eps_col[:, 0:1], EPS))
            step(nc.gpsimd.memset(eps_col[:, 1:2], GN_EPS))
            step(nc.gpsimd.memset(conv_groups[:, :], 0.0))
            step(nc.gpsimd.memset(conv_groups[0:64, 0:64], 1.0 / 64))
            step(nc.gpsimd.memset(conv_groups[64:128, 64:128], 1.0 / 64))
            for j in range(KC - 1):
                step(nc.gpsimd.memset(u_pad[:, :, j:j + 1], 0.0))
            pool.sem_inc(consts, 1)

        @block.tensor
        def _(pe):
            mm = nc.tensor.matmul

            def unit(key):
                n = unit_index[key]
                pe.wait_ge(ring_full[n % RING], 16 * (n // RING + 1))
                return ring[n % RING][:, :].rearrange("p (j f) -> p j f", j=KD)

            def wait_hT(which, j):
                pe.wait_ge(hT_act if j % 4 < 2 else hT_dve, which * KD // 2 + j // 4 * 2 + 2)

            pe.wait_ge(consts, 1)
            pe.wait_ge(rows_in, 16 * 4)
            nc.tensor.transpose(ps_fold[:, 0:(KC + 3) * CT4], small_rows[:, :],
                                ident[0:(KC + 3) * CT4, 0:(KC + 3) * CT4]).then_inc(smallT_done, 1)

            for t in range(TT):
                pe.wait_ge(xn_ready, t + 1)
                for j in range(KD):
                    dst = (ps_p if j < 4 else ps_q)[:, (j % 4) * S + t * P:(j % 4) * S + (t + 1) * P]
                    last = nc.tensor.transpose(dst, xn[:, t, j::KD], ident[:, :])
            last.then_inc(xT_done, 1)
            pe.wait_ge(c_ready, 1)

            def ada(u):
                w = unit(("ada", u))
                if u >= 1:
                    pe.wait_ge(part_read, u)
                for j in range(KD):
                    q = j % 4
                    last = mm(ps_part[32 * q:32 * q + 32, :], c_wide[:, j, :], w[:, j, :],
                              start=(j < 4), stop=(j >= 4))
                last.then_inc(part_done, 1)

            def fold_unit(u):
                pe.wait_ge(part_read, u + 1)
                if u == 0:
                    pe.wait_ge(smallT_read, 1)
                else:
                    pe.wait_ge(fold_read, u)
                vec, half = u // 2, u % 2
                if vec in (2, 5):
                    mm(ps_fold[:, :], fold[:, :], part[:, u % 2, :], start=True, stop=True).then_inc(fold_done, 1)
                else:
                    lo = 64 * half
                    for j in range(KD):
                        last = mm(ps_fold[lo:lo + 64, j:j + 1], part[:, u % 2, j::KD], fold[:, 0:1],
                                  start=True, stop=True)
                    last.then_inc(fold_done, 1)

            def win_tokens(k, dst):
                w = unit(("win", k))
                for t in range(TT):
                    for j in range(KD):
                        if k == 0 and t == 0:
                            wait_hT(0, j)
                        last = mm(dst[:, t * U:(t + 1) * U], hT[:, j, t * P:(t + 1) * P], w[:, j, :],
                                  start=(j == 0), stop=(j == KD - 1))
                last.then_inc(win_done, 1)

            def win_channels(k, dst):
                w = unit(("win", k))
                for m in range(CT4):
                    for j in range(KD):
                        last = mm(dst[:, m * S:(m + 1) * S], w[:, j, m * P:(m + 1) * P], hT[:, j, :],
                                  start=(j == 0), stop=(j == KD - 1))
                last.then_inc(win_done, 1)

            def turn(src, done):
                for m in range(CT4):
                    for t in range(TT):
                        last = nc.tensor.transpose(ps_s[:, m * S + t * P:m * S + (t + 1) * P],
                                                   src[:, t, m * P:(m + 1) * P], ident[:, :])
                last.then_inc(done, 1)

            def scores(h):
                lo = 64 * (h % 2)
                if h >= 2:
                    pe.wait_ge(weighted_ready, h - 1)
                dst = ps_s[:, (h % 2) * 512:(h % 2) * 512 + S + P]
                mm(dst[:, 0:S], kT[lo:lo + 64, h // 2, 0:P], qT[lo:lo + 64, h // 2, :], start=True, stop=True)
                mm(dst[:, S:S + P], kT[lo:lo + 64, h // 2, P:S], qT[lo:lo + 64, h // 2, P:S],
                   start=True, stop=True).then_inc(scores_done, 1)

            def apply_v(h):
                pe.wait_ge(weighted_ready, h + 1)
                w = weighted[:, h % 2, :]
                y0 = ps_p[:, h * DH:(h + 1) * DH]
                y1 = ps_p[:, RW + h * DH:RW + (h + 1) * DH]
                mm(y0, w[:, 0:P], v_sb[:, 0, h * DH:(h + 1) * DH], start=True, stop=True)
                mm(y1, w[:, P:S], v_sb[:, 0, h * DH:(h + 1) * DH], start=True, stop=False)
                mm(y1, w[:, S:S + P], v_sb[:, 1, h * DH:(h + 1) * DH], start=False, stop=True).then_inc(pv_done, 1)

            for u in range(4):
                ada(u)
                fold_unit(u)
            win_tokens(0, ps_p)
            ada(4)
            win_tokens(1, ps_q)
            fold_unit(4)
            ada(5)
            pe.wait_ge(q_ready, 2 * TT)
            win_tokens(2, ps_p)
            fold_unit(5)
            ada(6)
            turn(q_rot, qT_done)
            pe.wait_ge(k_ready, 2 * TT)
            win_tokens(3, ps_q)
            fold_unit(6)
            ada(7)
            pe.wait_ge(qT_ready, 1)
            turn(k_rot, kT_done)
            pe.wait_ge(v_ready, 1)
            win_channels(4, ps_p)
            fold_unit(7)
            ada(8)
            pe.wait_ge(kT_ready, 1)
            scores(0)
            scores(1)
            pe.wait_ge(g_ready, 1)
            win_channels(5, ps_q)
            fold_unit(8)
            ada(9)
            pe.wait_ge(b_ready, 1)
            apply_v(0)
            apply_v(1)
            scores(2)
            scores(3)
            pe.wait_ge(c_read, 1)
            win_channels(6, ps_q)
            fold_unit(9)
            ada(10)
            apply_v(2)
            apply_v(3)
            scores(4)
            scores(5)
            fold_unit(10)
            ada(11)
            apply_v(4)
            apply_v(5)
            scores(6)
            scores(7)
            fold_unit(11)
            apply_v(6)
            apply_v(7)
            pe.wait_ge(convsq_ready, 1)
            pe.wait_ge(u_ready, 1)
            for i in range(2):
                last = mm(ps_q[:, i * 512:(i + 1) * 512], conv_groups[:, :],
                          b_sb[:, 2 * i:2 * i + 2, :].rearrange("p m s -> p (m s)"), start=True, stop=True)
            last.then_inc(convms_done, 1)
            wo = [unit(("wout", 0)), unit(("wout", 1))]
            pe.wait_ge(yT_conv, 1)
            pe.wait_ge(weighted_ready, H)
            dst = [ps_s, ps_q]

            def project(n, t, k):
                return mm(dst[n][:, t * U:(t + 1) * U], yT[:, k, t * P:(t + 1) * P], wo[n][:, k, :],
                          start=(k == CT4), stop=(k == CT4 - 1))

            for n in range(2):
                for t in range(TT):
                    for k in range(CT4, KD):
                        project(n, t, k)
            pe.wait_ge(yret_ready, 1)
            pe.wait_ge(fold_read, 12)
            for m in range(CT4):
                for t in range(TT):
                    last = nc.tensor.transpose(ps_yT[:, m * S + t * P:m * S + (t + 1) * P],
                                               q_rot[:, t, m * P:(m + 1) * P], ident[:, :])
            last.then_inc(yretT_done, 1)
            pe.wait_ge(yT_ret, CT4)
            for t in range(TT):
                for n in range(2):
                    for k in range(CT4):
                        last = project(n, t, k)
                last.then_inc(wout_done, 1)

            for t in range(TT):
                pe.wait_ge(xn_ready, TT + t + 1)
                for j in range(KD):
                    d = banks(0, 4)[:, j * S + t * P:j * S + (t + 1) * P]
                    last = nc.tensor.transpose(d, xn[:, t, j::KD], ident[:, :])
            last.then_inc(xT_done, 1)
            pe.wait_ge(router_in, 16 * 4)
            pe.wait_ge(x1_ready, TT)
            for t in range(TT):
                for j in range(KD):
                    if t == 0:
                        wait_hT(1, j)
                    last = mm(ps_q[:, t * (G + E):(t + 1) * (G + E)], hT[:, j, t * P:(t + 1) * P],
                              router_w[:, j, :], start=(j == 0), stop=(j == KD - 1))
            last.then_inc(logits_done, 1)
            pe.wait_ge(mask_ready, 1)
            rank = ps_s[:, 0:TT * E]
            count = ps_s[:, 512:512 + E]
            mm(rank[:, 0:E], before[:, :], msk[:, 0, :], start=True, stop=True)
            mm(rank[:, E:2 * E], ones[:, :], msk[:, 0, :], start=True, stop=False)
            mm(rank[:, E:2 * E], before[:, :], msk[:, 1, :], start=False, stop=True)
            mm(count, ones[:, :], msk[:, 0, :], start=True, stop=False)
            mm(count, ones[:, :], msk[:, 1, :], start=False, stop=True).then_inc(rank_done, 1)

            pe.wait_ge(zero_ready, 3)
            for b in range(2 * TT):
                mm(ps_acc[:, b * 512:(b + 1) * 512], placeT[:, 0:P], y_sb[:, 0:512], start=True, stop=False,
                   skip_group_check=True)

            def gather(g1):
                pe.wait_ge(pick_ready, g1)
                for j in range(KD):
                    for t in range(TT):
                        last = mm(ps_xy[:, j * 2 * SLOTS:(j + 1) * 2 * SLOTS], xn[:, t, j::KD], pick[:, t, :],
                                  start=(t == 0), stop=(t == TT - 1))
                last.then_inc(gather_done, 1)

            def scatter(last_pair=False):
                for b in range(2 * TT):
                    t, n = b // 2, b % 2
                    last = mm(ps_acc[:, b * 512:(b + 1) * 512], placeT[:, t * P:(t + 1) * P],
                              y_sb[:, n * 512:(n + 1) * 512], start=False, stop=last_pair, skip_group_check=True)
                return last

            pe.wait_ge(npass_ready, 1)
            npass = pe.value_load(npass_i[0:1, 0:1], min_val=1, max_val=MAX_PASS)
            gather(1)
            with pe.Fori(0, npass * PAIRS) as g:
                pe.wait_ge(xg_lo, g + 1)
                pe.wait_ge(xg_hi, g + 1)
                pe.wait_ge(hidT_ready, g + 1)
                pe.wait_ge(gate_full[0], g * 16 + 16)
                pe.wait_ge(gate_full[1], g * 16 + 16)
                for j in range(KD):
                    for k in range(2):
                        last = mm(ps_gate[64 * k:64 * k + 64, :], xgT[:, j, 64 * k:64 * k + 64], gate_w[k][:, j, :],
                                  start=(j == 0), stop=(j == KD - 1))
                last.then_inc(gate_done, 1)
                pe.wait_ge(placeT_ready, g + 1)
                pe.wait_ge(up_full[0], g * 16 + 16)
                pe.wait_ge(up_full[1], g * 16 + 16)
                for j in range(KD):
                    for k in range(2):
                        last = mm(ps_up[64 * k:64 * k + 64, :], xgT[:, j, 64 * k:64 * k + 64], up_w[k][:, j, :],
                                  start=(j == 0), stop=(j == KD - 1))
                last.then_inc(up_done, 1)
                pe.wait_ge(y_lo, g + 1)
                pe.wait_ge(y_hi, g + 1)
                scatter()
                gather(g + 2)
                pe.wait_ge(hid_ready, g + 1)
                for j in range(KF):
                    nc.tensor.transpose(ps_gate[:, j * P:(j + 1) * P], hid[:, j::KF], ident[:, :])
                pe.wait_ge(place_ready, g + 1)
                for t in range(TT):
                    last = nc.tensor.transpose(ps_up[:, t * P:(t + 1) * P], place[:, t, :], ident[:, :])
                last.then_inc(turned, 1)
                pe.wait_ge(xg_lo, g + 2)
                pe.wait_ge(xg_hi, g + 2)
                pe.wait_ge(hidT_ready, g + 2)
                pe.wait_ge(down_full[0], g * 16 + 16)
                pe.wait_ge(down_full[1], g * 16 + 16)
                for n in range(2):
                    for j in range(KF):
                        for k in range(2):
                            last = mm(ps_xy[64 * k:64 * k + 64, n * 512:(n + 1) * 512], hidT[:, j, 64 * k:64 * k + 64],
                                      down_w[k][:, j, n * 512:(n + 1) * 512], start=(j == 0), stop=(j == KF - 1))
                last.then_inc(down_done, 1)
            pe.wait_ge(placeT_ready, npass * PAIRS + 1)
            pe.wait_ge(y_lo, npass * PAIRS + 1)
            pe.wait_ge(y_hi, npass * PAIRS + 1)
            scatter(True).then_inc(acc_done, 1)

        @block.scalar
        def _(act):
            steps = [0]

            def step(ins):
                ins.then_inc(act_step, 1)
                steps[0] += 1
                act.wait_ge(act_step, steps[0])

            act.dma_start(cvec[:, 0, :], c.rearrange("b (p j) -> (b p) j", p=P)).then_inc(c_in, 16)
            act.dma_start(x_sb[:, :, :], x.rearrange("b (t p) d -> (b p) t d", p=P)).then_inc(x_in, 16)
            act.dma_start(pos_i[:, :], positions.rearrange("b (t p) -> (b p) t", p=P),
                          allow_slow_non_contiguous=True).then_inc(pos_in, 16)
            act.dma_start(mod_bias[:, :, :], ada_b.rearrange("l (v p j) -> (l p) v j", v=6, p=P)).then_inc(mod_in, 16)
            act.dma_start(norm_g[:, 0, :], norm_mix_g.rearrange("l (p j) -> (l p) j", p=P)).then_inc(mod_in, 16)
            act.dma_start(norm_g[:, 1, :], norm_ffn_g.rearrange("l (p j) -> (l p) j", p=P)).then_inc(mod_in, 16)
            for i, rows in enumerate((beta_ret, beta_conv, conv_b)):
                act.dma_start(small_rows[i * CT4:(i + 1) * CT4, :],
                              rows.rearrange("l (t p) -> (l t) p", p=P)).then_inc(rows_in, 16)
            act.dma_start(small_rows[3 * CT4:(3 + KC) * CT4, :],
                          conv_w.rearrange("l k (t p) -> (l k t) p", p=P)).then_inc(rows_in, 16)
            act.dma_start(gate_mix[:, :], ada_b[0, 2 * D:3 * D].partition_broadcast(P)).then_inc(wide_in, 16)
            act.dma_start(gate_ffn[:, :], ada_b[0, 5 * D:6 * D].partition_broadcast(P)).then_inc(wide_in, 16)
            act.dma_start(final_g[:, :], norm_final_g[:].partition_broadcast(P)).then_inc(wide_in, 16)
            act.dma_start(router_w[:, :, 0:G],
                          router_group_w.rearrange("l (p j) g -> (l p) j g", p=P)).then_inc(router_in, 16)
            act.dma_start(router_w[:, :, G:G + E],
                          router_expert_w.rearrange("l (p j) g -> (l p) j g", p=P)).then_inc(router_in, 16)
            act.dma_start(router_b[:, 0:G], router_group_b[0, :].partition_broadcast(P)).then_inc(router_in, 16)
            act.dma_start(router_b[:, G:G + E], router_expert_b[0, :].partition_broadcast(P)).then_inc(router_in, 16)

            act.wait_ge(c_in, 16)
            nc.scalar.activation(cvec[:, 1, :], cvec[:, 0, :], ACT.Exp, scale=-1.0).then_inc(c_exp, 1)
            act.wait_ge(x_in, 16)
            for t in range(TT):
                nc.scalar.activation(xn[:, t, :], x_sb[:, t, :], ACT.Square,
                                     accum_out=ssq[:, 0, t:t + 1]).then_inc(squares, 1)
            act.wait_ge(squares, TT)
            act.wait_ge(consts, 1)
            nc.scalar.activation(rms[:, 0, :], ssq[:, 0, :], ACT.Sqrt, bias=eps_col[:, 0:1],
                                 scale=1.0 / D).then_inc(root_ready, 1)
            act.wait_ge(trig_arg_ready, 1)
            nc.scalar.activation(trig, trig_arg[:, 3], ACT.Sin).then_inc(trig_ready, 1)
            act.wait_ge(decay_ready, 1)
            for h in range(H):
                lg_h = float(np.log1p(-np.exp2(np.float32(-5.0 - h))).astype(np.float32))
                nc.scalar.activation(decay[:, h, :], dist, ACT.Exp, scale=lg_h).then_inc(decay_masked, 1)

            def part_copy(u):
                act.wait_ge(part_done, u + 1)
                if u >= 2:
                    act.wait_ge(fold_done, u - 1)
                nc.scalar.copy(part[:, u % 2, :], ps_part[:, :]).then_inc(part_read, 1)

            def hT_by_act(which, src):
                for j in (0, 1, 4, 5):
                    nc.scalar.activation(hT[:, j, :], src(j), ACT.Identity, scale=scale_a[:, which, j:j + 1],
                                         bias=modcol[:, 2 * which, j:j + 1]).then_inc(hT_act, 1)

            for u in range(4):
                part_copy(u)
            act.wait_ge(xT_done, 1)
            act.wait_ge(scales_ready, 1)
            hT_by_act(0, lambda j: (ps_p if j < 4 else ps_q)[:, (j % 4) * S:(j % 4 + 1) * S])
            part_copy(4)
            part_copy(5)
            act.wait_ge(win_done, 3)
            nc.scalar.copy(v_sb, ps_p.rearrange("p (t n) -> p t n", t=TT)).then_inc(v_ready, 1)
            part_copy(6)
            act.wait_ge(qT_done, 1)
            nc.scalar.copy(qT[:, :, :], ps_s.rearrange("p (m s) -> p m s", m=CT4)).then_inc(qT_ready, 1)
            act.wait_ge(win_done, 4)
            nc.scalar.activation(g_silu, ps_q.rearrange("p (t n) -> p t n", t=TT), ACT.Exp,
                                 scale=-1.0).then_inc(g_exp, 1)
            part_copy(7)
            act.wait_ge(kT_done, 1)
            nc.scalar.copy(kT, ps_s.rearrange("p (m s) -> p m s", m=CT4)).then_inc(kT_ready, 1)
            act.wait_ge(win_done, 5)
            nc.scalar.copy(b_sb, ps_p.rearrange("p (m s) -> p m s", m=CT4)).then_inc(b_ready, 1)
            part_copy(8)
            act.wait_ge(win_done, 6)
            nc.scalar.copy(conv_y[:, :, :], ps_q.rearrange("p (m s) -> p m s", m=CT4)).then_inc(c_read, 1)
            part_copy(9)
            part_copy(10)
            part_copy(11)
            act.wait_ge(convy_ready, 1)
            nc.scalar.activation(b_sb, conv_y[:, :, :], ACT.Square).then_inc(convsq_ready, 1)
            act.wait_ge(convms_done, 1)
            nc.scalar.activation(b_sb, ps_q.rearrange("p (m s) -> p m s", m=CT4), ACT.Sqrt,
                                 bias=eps_col[:, 0:1]).then_inc(convroot_ready, 1)
            act.wait_ge(centered, 1)
            nc.scalar.activation(k_rot, q_rot, ACT.Square).then_inc(centered_sq, 1)
            act.wait_ge(gnvar_ready, 1)
            nc.scalar.activation(groups[:, 2, :], groups[:, 1, :], ACT.Sqrt, bias=eps_col[:, 1:2],
                                 scale=1.0 / DH).then_inc(gnroot_ready, 1)
            act.wait_ge(yretT_done, 1)
            for m in range(CT4):
                nc.scalar.activation(yT[:, m, :], ps_yT[:, m * S:(m + 1) * S], ACT.Copy,
                                     scale=small_cols[:, m:m + 1]).then_inc(yT_ret, 1)
            for t in range(TT):
                act.wait_ge(x1_ready, t + 1)
                nc.scalar.activation(xn[:, t, :], x_sb[:, t, :], ACT.Square,
                                     accum_out=ssq[:, 1, t:t + 1]).then_inc(squares, 1)
                act.wait_ge(squares, TT + t + 1)
                nc.scalar.activation(rms[:, 1, t:t + 1], ssq[:, 1, t:t + 1], ACT.Sqrt, bias=eps_col[:, 0:1],
                                     scale=1.0 / D).then_inc(root_ready, 1)
            act.wait_ge(xT_done, 2)
            hT_by_act(1, lambda j: banks(0, 4)[:, j * S:(j + 1) * S])
            act.wait_ge(group_shift, 1)
            nc.scalar.activation(rt[:, 1, :, 0:G], rt[:, 0, :, 0:G], ACT.Exp).then_inc(group_exp, 1)
            act.wait_ge(expert_shift, 1)
            nc.scalar.activation(rt[:, 5, :, :], rt[:, 4, :, :], ACT.Exp).then_inc(expert_exp, 1)

            def gathered_lo(g1):
                act.wait_ge(gather_done, g1)
                for j in range(KD // 2):
                    last = nc.scalar.activation(xgT[:, j, :], ps_xy[:, j * P:(j + 1) * P], ACT.Identity,
                                                scale=scale_a[:, 1, j:j + 1], bias=modcol[:, 2, j:j + 1])
                last.then_inc(xg_lo, 1)

            act.wait_ge(npass_ready, 1)
            npass = act.value_load(npass_i[0:1, 0:1], min_val=1, max_val=MAX_PASS)
            gathered_lo(1)
            with act.Fori(0, npass * PAIRS) as g:
                act.wait_ge(gate_done, g + 1)
                nc.scalar.activation(ea, ps_gate, ACT.Exp, scale=-1.0).then_inc(ea_ready, 1)
                gathered_lo(g + 2)
                act.wait_ge(turned, g + 1)
                nc.scalar.copy(placeT, ps_up[:, 0:TT * P]).then_inc(placeT_ready, 1)
                act.wait_ge(down_done, g + 1)
                nc.scalar.copy(y_sb[:, 0:512], ps_xy[:, 0:512]).then_inc(y_lo, 1)

            for t in range(TT):
                act.wait_ge(x1_ready, TT + t + 1)
                nc.scalar.activation(xn[:, t, :], x_sb[:, t, :], ACT.Square,
                                     accum_out=ssq[:, 2, t:t + 1]).then_inc(squares, 1)
                act.wait_ge(squares, 2 * TT + t + 1)
                nc.scalar.activation(rms[:, 2, t:t + 1], ssq[:, 2, t:t + 1], ACT.Sqrt, bias=eps_col[:, 0:1],
                                     scale=1.0 / D).then_inc(root_ready, 1)
            out_rows = out.rearrange("b (t p) d -> t (b p) d", p=P)
            for t in range(TT):
                act.wait_ge(out_ready, t + 1)
                act.dma_start(out_rows[t], xn[:, t, :]).then_inc(out_written, 16)
            act.wait_ge(out_written, 16 * TT)

        @block.vector
        def _(dve):
            v = nc.vector
            steps = [0]

            def step(ins):
                ins.then_inc(dve_step, 1)
                steps[0] += 1
                dve.wait_ge(dve_step, steps[0])

            tt, ts, stt = v.tensor_tensor, v.tensor_scalar, v.scalar_tensor_tensor

            dve.wait_ge(c_exp, 1)
            step(ts(cvec[:, 2, :], cvec[:, 1, :], 1.0, None, ALU.add))
            step(v.reciprocal(cvec[:, 3, :], cvec[:, 2, :]))
            step(tt(cvec[:, 2, :], cvec[:, 3, :], cvec[:, 0, :], ALU.mult))
            v.tensor_copy(c_wide, cvec[:, 2, :].unsqueeze(2).broadcast_to([P, KD, 32])).then_inc(c_ready, 1)

            def norm_rows(which, t0, t1, ready, count):
                dve.wait_ge(root_ready, count)
                step(v.reciprocal(ssq[:, which, t0:t1], rms[:, which, t0:t1]))
                for t in range(t0, t1):
                    ts(xn[:, t, :], x_sb[:, t, :], ssq[:, which, t:t + 1], None, ALU.mult).then_inc(ready, 1)

            norm_rows(0, 0, TT, xn_ready, 1)
            dve.wait_ge(consts, 1)
            dve.wait_ge(pos_in, 16)
            step(v.tensor_copy(pos_f, pos_i[:, :]))
            angle, turns, red, arg = (trig_arg[:, i] for i in range(4))
            for t in range(TT):
                ts(angle[:, 1, t, :], inv_freq, pos_f[:, t:t + 1], None, ALU.mult).then_inc(dve_step, 1)
                steps[0] += 1
            dve.wait_ge(dve_step, steps[0])
            for i, quarter in ((0, 0.25), (1, 0.0)):
                step(ts(turns[:, i], angle[:, 1], 1.0 / TWO_PI, quarter, ALU.mult, ALU.add))
                step(ts(red[:, i], turns[:, i], ROUND, None, ALU.add))
                step(ts(turns[:, i], red[:, i], -ROUND, None, ALU.add))
                step(stt(red[:, i], turns[:, i], -TWO_PI_HI, angle[:, 1], ALU.mult, ALU.add))
                step(stt(arg[:, i], turns[:, i], -TWO_PI_MID, red[:, i], ALU.mult, ALU.add))
                step(stt(red[:, i], turns[:, i], -TWO_PI_LO, arg[:, i], ALU.mult, ALU.add))
                step(ts(turns[:, i], red[:, i], (1 - i) * np.pi / 2, -PI_BELOW, ALU.add, ALU.max))
                last = ts(arg[:, i], turns[:, i], PI_BELOW, None, ALU.min)
                if i == 0:
                    step(last)
            last.then_inc(trig_arg_ready, 1)
            stt(dist, dist, -1.0, dist, ALU.mult, ALU.max).then_inc(decay_ready, 1)
            dve.wait_ge(decay_masked, H)
            v.memset(decay[64:128, :, 0:64], 0.0).then_inc(dve_step, 1)
            steps[0] += 1
            dve.wait_ge(dve_step, steps[0])
            dve.wait_ge(smallT_done, 1)
            v.tensor_copy(small_cols[:, :], ps_fold[:, 0:(KC + 3) * CT4]).then_inc(smallT_read, 1)

            def fold_read_out(u):
                vec, half = u // 2, u % 2
                dve.wait_ge(fold_done, u + 1)
                if vec in (2, 5):
                    dst = (gate_mix if vec == 2 else gate_ffn)[:, half * U:(half + 1) * U]
                    tt(dst, ps_fold, dst, ALU.add).then_inc(fold_read, 1)
                else:
                    lo = 64 * half
                    tt(modcol[lo:lo + 64, {0: 0, 1: 1, 3: 2, 4: 3}[vec], :], ps_fold[lo:lo + 64, 0:KD],
                       mod_bias[lo:lo + 64, vec, :], ALU.add).then_inc(fold_read, 1)

            def scales(which, count):
                dve.wait_ge(fold_read, count)
                stt(scale_a[:, which, :], modcol[:, 2 * which + 1, :], 1.0, norm_g[:, which, :],
                    ALU.add, ALU.mult).then_inc(scales_ready, 1)

            def hT_by_dve(which, src):
                for j in (2, 3, 6, 7):
                    ts(hT[:, j, :], src(j), scale_a[:, which, j:j + 1], modcol[:, 2 * which, j:j + 1],
                       ALU.mult, ALU.add).then_inc(hT_dve, 1)

            dve.wait_ge(mod_in, 16 * 3)
            dve.wait_ge(wide_in, 16 * 3)
            for u in range(4):
                fold_read_out(u)
            scales(0, 4)
            dve.wait_ge(scales_ready, 1)
            dve.wait_ge(xT_done, 1)
            hT_by_dve(0, lambda j: (ps_p if j < 4 else ps_q)[:, (j % 4) * S:(j % 4 + 1) * S])
            dve.wait_ge(trig_ready, 1)

            def rotate(src, dst, ready):
                for t in range(TT):
                    s3 = src[:, t * RW:(t + 1) * RW].rearrange("p (a f) -> p a f", f=HALF)
                    cos = trig[:, 0, t, :].unsqueeze(1).broadcast_to([P, 2 * H, HALF])
                    sin = trig[:, 1, t, :].unsqueeze(1).broadcast_to([P, 2 * H, HALF])
                    if t:
                        dve.wait_ge(ready, 2 * t)
                    tt(tmp_c.rearrange("p (a f) -> p a f", f=HALF), s3, cos, ALU.mult).then_inc(dve_step, 1)
                    step_n()
                    step(tt(tmp_s.rearrange("p (a f) -> p a f", f=HALF), s3, sin, ALU.mult))
                    c4 = tmp_c.rearrange("p (h a f) -> p h a f", a=2, f=HALF)
                    s4 = tmp_s.rearrange("p (h a f) -> p h a f", a=2, f=HALF)
                    d4 = dst[:, t].rearrange("p (h a f) -> p h a f", a=2, f=HALF)
                    tt(d4[:, :, 0, :], c4[:, :, 0, :], s4[:, :, 1, :], ALU.subtract).then_inc(ready, 1)
                    tt(d4[:, :, 1, :], c4[:, :, 1, :], s4[:, :, 0, :], ALU.add).then_inc(ready, 1)

            def step_n():
                steps[0] += 1

            dve.wait_ge(win_done, 1)
            rotate(ps_p, q_rot, q_ready)
            dve.wait_ge(q_ready, 2 * TT)
            dve.wait_ge(win_done, 2)
            rotate(ps_q, k_rot, k_ready)
            fold_read_out(4)
            fold_read_out(5)
            dve.wait_ge(g_exp, 1)
            g2 = ps_q.rearrange("p (t n) -> p t n", t=TT)
            step(ts(g_silu, g_silu, 1.0, None, ALU.add))
            step(v.reciprocal(g_silu, g_silu))
            tt(g_silu, g_silu, g2, ALU.mult).then_inc(g_ready, 1)
            fold_read_out(6)
            fold_read_out(7)

            def weigh(h):
                dve.wait_ge(scores_done, h + 1)
                if h >= 2:
                    dve.wait_ge(pv_done, h - 1)
                src = ps_s[:, (h % 2) * 512:(h % 2) * 512 + S + P]
                stt(weighted[:, h % 2, 0:S], src[:, 0:S], DH ** -0.5, decay[:, h, :],
                    ALU.mult, ALU.mult).then_inc(dve_step, 1)
                step_n()
                stt(weighted[:, h % 2, S:S + P], src[:, S:S + P], DH ** -0.5, decay[:, h, 0:P],
                    ALU.mult, ALU.mult).then_inc(weighted_ready, 1)

            taps = small_cols[:, 3 * CT4:(3 + KC) * CT4].rearrange("p (k m) -> p k m", k=KC)

            def conv(m):
                step(ts(conv_y[:, m, :], u_pad[:, m, KC - 1:KC - 1 + S], taps[:, KC - 1, m:m + 1],
                        small_cols[:, 2 * CT4 + m:2 * CT4 + m + 1], ALU.mult, ALU.add))
                for k in range(KC - 1):
                    step(stt(conv_y[:, m, :], u_pad[:, m, k:k + S], taps[:, k, m:m + 1], conv_y[:, m, :],
                             ALU.mult, ALU.add))

            weigh(0)
            weigh(1)
            fold_read_out(8)
            weigh(2)
            weigh(3)
            dve.wait_ge(win_done, 7)
            dve.wait_ge(c_read, 1)
            tt(u_pad[:, :, KC - 1:KC - 1 + S], conv_y[:, :, :], ps_q.rearrange("p (m s) -> p m s", m=CT4),
               ALU.mult).then_inc(u_ready, 1)
            fold_read_out(9)
            weigh(4)
            weigh(5)
            fold_read_out(10)
            dve.wait_ge(u_ready, 1)
            conv(0)
            conv(1)
            weigh(6)
            weigh(7)
            fold_read_out(11)
            conv(2)
            conv(3)
            dve.wait_ge(b_ready, 1)
            tt(conv_y[:, :, :], conv_y[:, :, :], b_sb, ALU.mult).then_inc(convy_ready, 1)
            scales(1, 12)

            dve.wait_ge(pv_done, H)
            y3 = ps_p.rearrange("p (a f) -> p a f", f=DH)
            q3 = q_rot.rearrange("p t (h f) -> p (t h) f", f=DH)
            k3 = k_rot.rearrange("p t (h f) -> p (t h) f", f=DH)
            g3 = g_silu.rearrange("p t (h f) -> p (t h) f", f=DH)

            def per_head(ap):
                return ap.unsqueeze(2).broadcast_to([P, TT * H, DH])

            step(v.tensor_reduce(groups[:, 0, :], y3, AX.X, ALU.add))
            step(ts(groups[:, 1, :], groups[:, 0, :], 1.0 / DH, None, ALU.mult))
            dve.wait_ge(qT_done, 1)
            tt(q3, y3, per_head(groups[:, 1, :]), ALU.subtract).then_inc(centered, 1)
            dve.wait_ge(convroot_ready, 1)
            step(v.reciprocal(b_sb, b_sb))
            for m in range(CT4):
                last = stt(yT[:, CT4 + m, :], conv_y[:, m, :], small_cols[:, CT4 + m:CT4 + m + 1], b_sb[:, m, :],
                           ALU.mult, ALU.mult)
            last.then_inc(yT_conv, 1)
            dve.wait_ge(centered_sq, 1)
            v.tensor_reduce(groups[:, 1, :], k3, AX.X, ALU.add).then_inc(gnvar_ready, 1)
            step(tt(g3, g3, q3, ALU.mult))
            dve.wait_ge(gnroot_ready, 1)
            step(v.reciprocal(groups[:, 0, :], groups[:, 2, :]))
            tt(q3, g3, per_head(groups[:, 0, :]), ALU.mult).then_inc(yret_ready, 1)

            dve.wait_ge(fold_read, 12)
            for t in range(TT):
                dve.wait_ge(wout_done, t + 1)
                for n, src in ((0, ps_s), (1, ps_q)):
                    tt(xn[:, t, n * U:(n + 1) * U], src[:, t * U:(t + 1) * U], gate_mix[:, n * U:(n + 1) * U],
                       ALU.mult).then_inc(dve_step, 1)
                    step_n()
                dve.wait_ge(dve_step, steps[0])
                tt(x_sb[:, t, :], x_sb[:, t, :], xn[:, t, :], ALU.add).then_inc(x1_ready, 1)
            for t in range(TT):
                dve.wait_ge(x1_ready, t + 1)
                norm_rows(1, t, t + 1, xn_ready, 2 + t)
            dve.wait_ge(scales_ready, 2)
            dve.wait_ge(xT_done, 2)
            hT_by_dve(1, lambda j: banks(0, 4)[:, j * S:(j + 1) * S])

            dve.wait_ge(logits_done, 1)
            dve.wait_ge(router_in, 16 * 4)

            def wide(ap, n):
                return ap.broadcast_to([P, TT, n])

            step(tt(lg, ps_q[:, 0:TT * (G + E)].rearrange("p (t n) -> p t n", t=TT),
                    router_b[:, :].unsqueeze(1).broadcast_to([P, TT, G + E]), ALU.add))
            glg, elg = lg[:, :, 0:G], lg[:, :, G:G + E].rearrange("p t (g e) -> p t g e", g=G)
            col = lambda i: rt[:, 15, :, i:i + 1]
            step(v.tensor_reduce(col(0), glg, AX.X, ALU.max))
            tt(rt[:, 0, :, 0:G], glg, wide(col(0), G), ALU.subtract).then_inc(group_shift, 1)
            dve.wait_ge(group_exp, 1)

            def first_max(probs, n, top, work, onehot):
                step(v.tensor_reduce(top, probs, AX.X, ALU.max))
                step(tt(work, probs, wide(top, n), ALU.is_equal))
                step(tt(work, work, rev[:, EG - n:EG].unsqueeze(1).broadcast_to([P, TT, n]), ALU.mult))
                step(v.tensor_reduce(col(7), work, AX.X, ALU.max))
                step(tt(onehot, work, wide(col(7), n), ALU.is_equal))

            gp = rt[:, 1, :, 0:G]
            group_hot = rt[:, 3, :, 0:G]
            first_max(gp, G, col(1), rt[:, 2, :, 0:G], group_hot)
            step(v.tensor_reduce(col(2), gp, AX.X, ALU.add))
            ohe4 = ohe.rearrange("p t (g e) -> p t g e", g=G)
            step(tt(ohe4, elg, group_hot.unsqueeze(3).broadcast_to([P, TT, G, EG]), ALU.mult))
            step(v.tensor_reduce(rt[:, 6, :, :], ohe.rearrange("p t (g e) -> p t e g", g=G), AX.X, ALU.add))
            step(v.tensor_reduce(col(0), rt[:, 6, :, :], AX.X, ALU.max))
            tt(rt[:, 4, :, :], rt[:, 6, :, :], wide(col(0), EG), ALU.subtract).then_inc(expert_shift, 1)
            dve.wait_ge(expert_exp, 1)
            first_max(rt[:, 5, :, :], EG, col(3), rt[:, 7, :, :], rt[:, 8, :, :])
            step(stt(rt[:, 9, :, :], rt[:, 8, :, :], -4.0, rt[:, 5, :, :], ALU.mult, ALU.add))
            first_max(rt[:, 9, :, :], EG, col(4), rt[:, 7, :, :], rt[:, 10, :, :])
            step(tt(within8[:, 1], rt[:, 8, :, :], rt[:, 10, :, :], ALU.add))
            gh4 = group_hot.unsqueeze(3).broadcast_to([P, TT, G, EG])

            def spread(i):
                return within8[:, i].unsqueeze(2).broadcast_to([P, TT, G, EG])

            tt(msk.rearrange("p t (g e) -> p t g e", g=G), spread(1), gh4, ALU.mult).then_inc(mask_ready, 1)
            step(tt(col(5), col(3), col(4), ALU.add))
            step(tt(col(6), col(5), col(2), ALU.mult))
            step(v.reciprocal(col(5), col(6)))
            step(tt(col(6), col(5), col(1), ALU.mult))
            step(tt(col(0), col(3), col(6), ALU.mult))
            step(tt(col(5), col(4), col(6), ALU.mult))
            step(tt(rt[:, 11, :, :], rt[:, 8, :, :], wide(col(0), EG), ALU.mult))
            step(tt(rt[:, 12, :, :], rt[:, 10, :, :], wide(col(5), EG), ALU.mult))
            step(tt(within8[:, 0], rt[:, 11, :, :], rt[:, 12, :, :], ALU.add))
            step(tt(combine[:, :, :].rearrange("p t (g e) -> p t g e", g=G), spread(0), gh4, ALU.mult))
            dve.wait_ge(mask_ready, 1)
            dve.wait_ge(rank_done, 1)
            step(v.tensor_reduce(cnt[:, 0:1], ps_s[:, 512:512 + E], AX.X, ALU.max))
            step(ts(rt[0:1, 13, 0, 0:MAX_PASS], slot_ids[0:1, 0:MAX_PASS * SLOTS:SLOTS], cnt[0:1, 0:1], None,
                    ALU.is_lt))
            step(v.tensor_reduce(cnt[0:1, 1:2], rt[0:1, 13, 0, 0:MAX_PASS], AX.X, ALU.add))
            v.tensor_copy(npass_i[0:1, 0:1], cnt[0:1, 1:2]).then_inc(npass_ready, 1)
            step(stt(ohe, ps_s[:, 0:TT * E].rearrange("p (t e) -> p t e", t=TT), 1.0, msk, ALU.add, ALU.mult))
            step(ts(posm[:, :, :], ohe, -1.0, None, ALU.add))

            dve.wait_ge(yret_ready, 1)
            v.memset(placeT, 0.0).then_inc(zero_ready, 1)
            v.memset(y_sb[:, 0:512], 0.0).then_inc(zero_ready, 1)
            v.memset(y_sb[:, 512:1024], 0.0).then_inc(zero_ready, 1)
            dve.wait_ge(zero_ready, 3)
            dve.sem_inc(y_lo, 1)
            dve.sem_inc(y_hi, 1)
            dve.sem_inc(placeT_ready, 1)
            dve.sem_inc(hidT_ready, 1)

            def pick_pair(g, e, first):
                for k in range(2):
                    for t in range(TT):
                        last = ts(pick[:, t, k * SLOTS:(k + 1) * SLOTS], slot_ids[:, first],
                                  posm[:, t, bass.ds(e + k, 1)], None, ALU.is_equal)
                last.then_inc(pick_ready, 1)

            def gathered_hi(g1):
                dve.wait_ge(gather_done, g1)
                for j in range(KD // 2, KD):
                    last = ts(xgT[:, j, :], ps_xy[:, j * P:(j + 1) * P], scale_a[:, 1, j:j + 1],
                              modcol[:, 2, j:j + 1], ALU.mult, ALU.add)
                last.then_inc(xg_hi, 1)

            dve.wait_ge(npass_ready, 1)
            npass = dve.value_load(npass_i[0:1, 0:1], min_val=1, max_val=MAX_PASS)
            pick_pair(0, 0, slice(0, SLOTS))
            gathered_hi(1)
            with dve.Fori(0, npass * PAIRS) as g:
                e = (g % PAIRS) * 2
                for k in range(2):
                    for t in range(TT):
                        last = ts(place[:, t, k * SLOTS:(k + 1) * SLOTS],
                                  slot_ids[:, bass.ds((g // PAIRS) * SLOTS, SLOTS)],
                                  posm[:, t, bass.ds(e + k, 1)], combine[:, t, bass.ds(e + k, 1)],
                                  ALU.is_equal, ALU.mult)
                last.then_inc(place_ready, 1)
                pick_pair(g + 1, ((g + 1) % PAIRS) * 2, bass.ds(((g + 1) // PAIRS) * SLOTS, SLOTS))
                dve.wait_ge(ea_ready, g + 1)
                base = steps[0]
                ts(hid, ea, 1.0, None, ALU.add).then_inc(dve_step, 1)
                dve.wait_ge(dve_step, g * 3 + (base + 1))
                v.reciprocal(ea, hid).then_inc(dve_step, 1)
                dve.wait_ge(dve_step, g * 3 + (base + 2))
                tt(hid, ea, ps_gate, ALU.mult).then_inc(dve_step, 1)
                dve.wait_ge(dve_step, g * 3 + (base + 3))
                dve.wait_ge(up_done, g + 1)
                tt(hid, hid, ps_up, ALU.mult).then_inc(hid_ready, 1)
                gathered_hi(g + 2)
                dve.wait_ge(turned, g + 1)
                v.tensor_copy(hidT, ps_gate.rearrange("p (j s) -> p j s", j=KF)).then_inc(hidT_ready, 1)
                dve.wait_ge(down_done, g + 1)
                v.tensor_copy(y_sb[:, 512:1024], ps_xy[:, 512:1024]).then_inc(y_hi, 1)

            dve.wait_ge(acc_done, 1)
            for t in range(TT):
                tt(xn[:, t, :], ps_acc[:, t * D:(t + 1) * D], gate_ffn[:, :], ALU.mult).then_inc(xn_ready, 1)
            for t in range(TT):
                dve.wait_ge(xn_ready, 2 * TT + t + 1)
                tt(x_sb[:, t, :], x_sb[:, t, :], xn[:, t, :], ALU.add).then_inc(x1_ready, 1)
            for t in range(TT):
                dve.wait_ge(root_ready, 4 + t)
                v.reciprocal(ssq[:, 3, t:t + 1], rms[:, 2, t:t + 1]).then_inc(npass_ready, 1)
                dve.wait_ge(npass_ready, t + 2)
                stt(xn[:, t, :], x_sb[:, t, :], ssq[:, 3, t:t + 1], final_g[:, :],
                    ALU.mult, ALU.mult).then_inc(out_ready, 1)


_INS = ["x", "c", "positions", "ada_w", "ada_b", "norm_mix_g", "norm_ffn_g", "w_in", "conv_w", "conv_b", "beta_ret",
        "beta_conv", "w_out", "router_group_w", "router_group_b", "router_expert_w", "router_expert_b",
        "expert_w_gate", "expert_w_up", "expert_w_down", "norm_final_g"]


def kernel(**inputs):
    import numpy as _np
    import concourse.bacc as _bacc
    from concourse import mybir as _mybir
    from concourse.bass_utils import run_bass_kernel_spmd as _run

    nc = _bacc.Bacc("TRN2", target_bir_lowering=False, num_devices=1)
    arrays, args = {}, []
    for name in _INS:
        a = _np.ascontiguousarray(inputs[name])
        arrays[f"in_{name}"] = a
        args.append(nc.dram_tensor(f"in_{name}", a.shape, _mybir.dt.from_np(a.dtype), kind="ExternalInput").ap())
    out = nc.dram_tensor("out_0", inputs["x"].shape, F32, kind="ExternalOutput").ap()
    hybrid_retention_moe_layer(nc, *args, out)
    r = _run(nc, [arrays], core_ids=[0])
    return r.results[0]["out_0"]
```

```python
from contextlib import ExitStack

import concourse.bass as bass
import numpy as np
from concourse import mybir

F32 = mybir.dt.float32
I32 = mybir.dt.int32
ALU = mybir.AluOpType
ACT = mybir.ActivationFunctionType
AX = mybir.AxisListType

P = 128
EPS = 1e-6
GN_EPS = 1e-5
ROPE_BASE = 10000.0
TWO_PI = 2.0 * np.pi
PI_BELOW = 3.1415925
TWO_PI_HI = 6.28125
TWO_PI_MID = float(np.float32(0.0019350051879882812))
TWO_PI_LO = float(np.float32(TWO_PI - TWO_PI_HI - TWO_PI_MID))
ROUND = 12582912.0
SLOTS = 64
RING = 6


def hybrid_retention_moe_layer(nc, x, c, positions, ada_w, ada_b, norm_mix_g, norm_ffn_g, w_in, conv_w, conv_b,
                               beta_ret, beta_conv, w_out, router_group_w, router_group_b, router_expert_w,
                               router_expert_b, expert_w_gate, expert_w_up, expert_w_down, norm_final_g, out):
    _, S, D = x.shape
    TT = S // P
    KD = D // P
    CHUNK = 64
    RW = D // 2
    H = 8
    DH = RW // H
    HALF = DH // 2
    CT4 = RW // P
    KC = conv_w.shape[1]
    G = router_group_w.shape[2]
    EG = expert_w_gate.shape[2]
    E = G * EG
    F = expert_w_gate.shape[4]
    KF = F // P
    PAIRS = E // 2
    U = 512
    MAX_PASS = S // SLOTS
    assert S == 256 and D == 1024 and RW == 512 and F == 512 and DH == CHUNK == 64

    gate_rows = expert_w_gate.rearrange("l g e (p j) f -> (l g e) p (j f)", p=P)
    up_rows = expert_w_up.rearrange("l g e (p j) f -> (l g e) p (j f)", p=P)
    down_rows = expert_w_down.rearrange("l g e (p j) f -> (l g e) p (j f)", p=P)
    ada_rows = ada_w.rearrange("l (p j) n -> (l p) j n", p=P)
    win_rows = w_in.rearrange("l (p j) n -> (l p) j n", p=P)
    wout_rows = w_out.rearrange("l (t p) n -> (l p) t n", p=P)

    units = [("ada", u) for u in range(4)]
    column_sets = ("q", "k", "v", "g", "b", "c", "h")
    used = ("q", "k", "h", "c", "b", "g", "v")
    for i, name in enumerate(used):
        units += [("win", column_sets.index(name))] + ([("ada", 4 + i)] if i < 6 else [])
    win_turn = {name: i + 1 for i, name in enumerate(used)}
    units += [("wout", 0), ("wout", 1), ("ada", 10), ("ada", 11)]
    BY_DVE = range(4, 10)
    unit_index = {key: n for n, key in enumerate(units)}
    NU = len(units)

    with ExitStack() as ctx:
        def sb(name, shape, dt=F32):
            return ctx.enter_context(nc.sbuf_tensor(name, shape, dt))

        def sem(name):
            return ctx.enter_context(nc.semaphore(name))

        ring = [sb(f"ring{i}", [P, KD * U]) for i in range(RING)]
        expert_slot = [ring[(NU + k) % RING] for k in range(6)]
        last_w = [expert_slot[k][:, :].rearrange("p (j d) -> p j d", j=KF) for k in (0, 1)]
        down_w = [expert_slot[k][:, :].rearrange("p (j d) -> p j d", j=KF) for k in (4, 5)]

        xn = sb("xn", [P, TT, D])

        late_gate = sb("late_gate", [P, 2, KD * F])
        conv_y = late_gate[:, 0, 0:CT4 * S].rearrange("p (m s) -> p m s", m=CT4)
        qT = late_gate[:, 0, CT4 * S:2 * CT4 * S].rearrange("p (m s) -> p m s", m=CT4)
        gate_mix = late_gate[:, 0, 2 * CT4 * S:2 * CT4 * S + D]
        spare = 2 * CT4 * S + D
        small_rows = late_gate[0:(KC + 3) * CT4, 0, spare:spare + P]
        groups = late_gate[:, 0, spare + P:spare + P + 3 * TT * H].rearrange("p (i a) -> p i a", i=3)
        hT = late_gate[:, 1, 0:KD * S].rearrange("p (j s) -> p j s", j=KD)
        x_sb = late_gate[:, 1, KD * S:KD * S + TT * D].rearrange("p (t d) -> p t d", t=TT)
        yT_ret_half = hT[:, 0:CT4, :]
        gate_ffn = sb("gate_ffn", [P, D])
        final_g = sb("final_g", [P, D])
        ident = sb("ident", [P, P])
        before = sb("before", [P, P])
        ones = sb("ones", [P, P])
        fold = sb("fold", [P, P])
        conv_groups = sb("conv_groups", [P, P])
        slot_ids = sb("slot_ids", [P, (MAX_PASS + 1) * SLOTS])
        rev = sb("rev", [P, EG])
        eps_col = sb("eps_col", [P, 2])
        router_w = sb("router_w", [P, KD, G + E])
        router_b = sb("router_b", [G + E, 1])
        mod_bias = sb("mod_bias", [P, 6, KD])
        norm_g = sb("norm_g", [P, 2, KD])
        modcol = sb("modcol", [P, 4, KD])
        scale_a = sb("scale_a", [P, 2, KD])
        small_cols = sb("small_cols", [P, (KC + 3) * CT4])
        mean_sq = sb("mean_sq", [P, 3, TT, 3])
        rms = sb("rms", [P, 3, TT])
        inv_rms = sb("inv_rms", [P, 3, TT])
        part = sb("part", [P, 2, U])
        posm = sb("posm", [P, TT, E])
        combine = sb("combine", [P, TT, E])
        more_i = sb("more_i", [1, 1], I32)

        x_flat = xn[:, :, :].rearrange("p t d -> p (t d)")
        ARENA = 12640
        arena = sb("arena", [P, ARENA])
        taken = [0]

        def front(shape):
            n = int(np.prod(shape))
            ap = arena[:, taken[0]:taken[0] + n]
            taken[0] += n
            assert taken[0] <= ARENA
            if len(shape) == 1:
                return ap
            names = "abcd"[:len(shape)]
            return ap.rearrange("p (%s) -> p %s" % (" ".join(names), " ".join(names)),
                                **{k: v for k, v in zip(names, shape)})

        decay = front([H, S])
        kT = front([CT4, S])
        g_raw = front([TT, RW])
        tmp_c, tmp_s = g_raw[:, 0], g_raw[:, 1]
        assert taken[0] == KD * F
        b_sb = front([CT4, S])
        v_sb = front([TT, RW])
        u_pad = front([CT4, S + KC - 1])
        cvec = front([4, KD])
        trig = front([2, TT, HALF])
        trig_arg = front([4, 2, TT, HALF])
        inv_freq = front([HALF])
        pos_f = front([TT])
        dist = front([S])
        taken[0] = 2 * KD * F
        wide_rows = arena[0:1, taken[0]:taken[0] + 3 * D]
        q_rot = front([TT, RW])
        k_rot = front([TT, RW])
        g_silu = front([TT, RW])
        scored = front([3, S + P])
        weighted = [x_flat[:, h * (S + P):(h + 1) * (S + P)] for h in range(5)] + [scored[:, h] for h in range(3)]
        c_wide_flat = sb("c_wide", [P, KD * 32])
        c_wide = c_wide_flat[:, :].rearrange("p (j c) -> p j c", j=KD)
        lgT = sb("lgT", [G + E, S])
        rt = sb("rt", [P, 16, TT, EG])
        within8 = sb("within8", [P, 2, TT, EG])
        msk = sb("msk", [P, TT, E])
        ohe = sb("ohe", [P, TT, E])
        cnt = sb("cnt", [P, 4])
        pos_i = sb("pos_i", [P, TT], I32)

        late_up = arena[:, 0:2 * KD * F].rearrange("p (k n) -> p k n", k=2)
        up_slot = [[expert_slot[k][:, :] for k in (0, 1)], [late_up[:, k, :] for k in (0, 1)]]
        gate_slot = [[expert_slot[k][:, :] for k in (2, 3)], [late_gate[:, k, :] for k in (0, 1)]]
        gate_w = [[ap.rearrange("p (j f) -> p j f", j=KD) for ap in pair] for pair in gate_slot]
        up_w = [[ap.rearrange("p (j f) -> p j f", j=KD) for ap in pair] for pair in up_slot]
        taken[0] = 2 * KD * F
        xgT = front([KD, 2 * SLOTS])
        pick = front([TT, 2 * SLOTS])
        place = front([TT, 2 * SLOTS])
        placeT = front([TT * P])
        gate_fold = arena[:, taken[0]:taken[0] + D]
        hid = front([F])
        ea = front([F])
        hidT = front([KF, 2 * SLOTS])
        y_sb = front([D])

        ps = ctx.enter_context(nc.psum_tensor("ps", [P, 8, 512], F32))

        def banks(a, n):
            return ps[:, a:a + n, :].rearrange("p b c -> p (b c)")

        ps_part = banks(0, 1)
        ps_fold = banks(1, 1)
        ps_p = banks(2, 2)
        ps_q = banks(4, 2)
        ps_s = banks(6, 2)
        ps_yT = banks(0, 2)
        ps_acc = banks(0, 4)
        acc = ps_acc.rearrange("p (t d) -> p t d", t=TT)
        ps_xy = banks(4, 2)
        ps_gate = banks(6, 1)
        ps_up = banks(7, 1)

        ring_full = [sem(f"ring_full{i}") for i in range(RING)]
        up_full = [[sem(f"up_full{h}{k}") for k in range(2)] for h in range(2)]
        gate_full = [[sem(f"gate_full{h}{k}") for k in range(2)] for h in range(2)]
        down_full = [sem("down_full0"), sem("down_full1")]
        last_full = [[sem(f"last_full{n}{k}") for k in range(2)] for n in range(2)]
        gate_done = sem("gate_done")
        up_done = sem("up_done")
        down_done = sem("down_done")
        x_in = sem("x_in")
        c_in = sem("c_in")
        pos_in = sem("pos_in")
        mod_in = sem("mod_in")
        rows_in = sem("rows_in")
        router_in = sem("router_in")
        wide_in = sem("wide_in")
        wide_ready = sem("wide_ready")
        h_read = sem("h_read")
        g_read = sem("g_read")
        logitsT_done = sem("logitsT_done")
        logitsT_ready = sem("logitsT_ready")
        last_step = sem("last_step")
        out_written = sem("out_written")
        consts = sem("consts")
        act_step = sem("act_step")
        dve_step = sem("dve_step")
        pool_step = sem("pool_step")
        c_exp = sem("c_exp")
        c_ready = sem("c_ready")
        squares = sem("squares")
        rms_ready = sem("rms_ready")
        root_ready = sem("root_ready")
        xn_ready = sem("xn_ready")
        trig_arg_ready = sem("trig_arg_ready")
        trig_ready = sem("trig_ready")
        decay_ready = sem("decay_ready")
        decay_masked = sem("decay_masked")
        xT_done = sem("xT_done")
        part_done = sem("part_done")
        part_read = sem("part_read")
        fold_done = sem("fold_done")
        fold_read = sem("fold_read")
        smallT_done = sem("smallT_done")
        smallT_read = sem("smallT_read")
        scales_ready = sem("scales_ready")
        hT_act = sem("hT_act")
        hT_dve = sem("hT_dve")
        win_done = sem("win_done")
        q_ready = sem("q_ready")
        k_ready = sem("k_ready")
        v_ready = sem("v_ready")
        g_exp = sem("g_exp")
        g_ready = sem("g_ready")
        b_ready = sem("b_ready")
        c_read = sem("c_read")
        u_ready = sem("u_ready")
        qT_done = sem("qT_done")
        qT_ready = sem("qT_ready")
        kT_done = sem("kT_done")
        kT_ready = sem("kT_ready")
        scores_done = sem("scores_done")
        weighted_ready = sem("weighted_ready")
        pv_done = sem("pv_done")
        convy_ready = sem("convy_ready")
        convsq_ready = sem("convsq_ready")
        convms_done = sem("convms_done")
        convroot_ready = sem("convroot_ready")
        yT_conv = sem("yT_conv")
        centered = sem("centered")
        centered_sq = sem("centered_sq")
        gnvar_ready = sem("gnvar_ready")
        gnroot_ready = sem("gnroot_ready")
        yret_ready = sem("yret_ready")
        yretT_done = sem("yretT_done")
        yT_ret = sem("yT_ret")
        wout_done = sem("wout_done")
        x1_ready = sem("x1_ready")
        logits_done = sem("logits_done")
        group_shift = sem("group_shift")
        group_exp = sem("group_exp")
        expert_shift = sem("expert_shift")
        expert_exp = sem("expert_exp")
        mask_ready = sem("mask_ready")
        rank_done = sem("rank_done")
        more_ready = sem("more_ready")
        zero_ready = sem("zero_ready")
        pick_ready = sem("pick_ready")
        place_ready = sem("place_ready")
        gather_done = sem("gather_done")
        xg_lo = sem("xg_lo")
        xg_hi = sem("xg_hi")
        ea_ready = sem("ea_ready")
        hid_ready = sem("hid_ready")
        turned = sem("turned")
        hidT_ready = sem("hidT_ready")
        placeT_ready = sem("placeT_ready")
        y_ready = sem("y_ready")
        gate_ready = sem("gate_ready")
        acc_open = sem("acc_open")
        acc_done = sem("acc_done")
        out_ready = sem("out_ready")

        block = ctx.enter_context(nc.Block())

        def expert_view(ap, e):
            return ap[bass.ds(e, 1)].rearrange("e p n -> p (e n)")

        def yT(k):
            return yT_ret_half[:, k, :] if k < CT4 else qT[:, k - CT4, :]

        def unit_used(n):
            kind, u = units[n]
            if kind == "win":
                return win_done, win_turn[column_sets[u]]
            if kind == "wout":
                return wout_done, (u + 1) * TT
            if u in BY_DVE:
                return part_read, u + 1
            return part_done, u + 1 if u < BY_DVE[0] else u + 1 - len(BY_DVE)

        @block.sync
        def _(sp):
            sp.dma_start(cvec[:, 0, :], c.rearrange("b (p j) -> (b p) j", p=P)).then_inc(c_in, 16)
            sp.dma_start(mod_bias[:, :, :], ada_b.rearrange("l (v p j) -> (l p) v j", v=6, p=P)).then_inc(mod_in, 16)
            sp.dma_start(norm_g[:, 0, :], norm_mix_g.rearrange("l (p j) -> (l p) j", p=P)).then_inc(mod_in, 16)
            sp.dma_start(norm_g[:, 1, :], norm_ffn_g.rearrange("l (p j) -> (l p) j", p=P)).then_inc(mod_in, 16)
            sp.dma_start(x_sb[:, :, :], x.rearrange("b (t p) d -> (b p) t d", p=P)).then_inc(x_in, 16)
            for n, (kind, u) in enumerate(units):
                if n >= RING:
                    sp.wait_ge(*unit_used(n - RING))
                rows = {"ada": ada_rows, "win": win_rows, "wout": wout_rows}[kind]
                sp.dma_start(ring[n % RING][:, :].rearrange("p (j f) -> p j f", j=KD),
                             rows[:, :, u * U:(u + 1) * U]).then_inc(ring_full[n % RING], 16)
            def load_first(k, rows, full):
                sp.wait_ge(*unit_used(NU - RING + k))
                sp.dma_start(expert_slot[k][:, :], rows[k % 2]).then_inc(full[k % 2], 16)

            load_first(0, up_rows, up_full[0])
            sp.wait_ge(weighted_ready, H)
            sp.wait_ge(g_ready, 1)
            sp.dma_start(up_slot[1][0], up_rows[2]).then_inc(up_full[1][0], 16)
            load_first(1, up_rows, up_full[0])
            sp.wait_ge(pv_done, H)
            sp.wait_ge(yT_conv, 1)
            sp.dma_start(up_slot[1][1], up_rows[3]).then_inc(up_full[1][1], 16)
            for k in range(2, 4):
                load_first(k, gate_rows, gate_full[0])
            load_first(4, down_rows, down_full)
            sp.wait_ge(x1_ready, 2 * TT)
            sp.dma_start(gate_slot[1][0], gate_rows[2]).then_inc(gate_full[1][0], 16)
            load_first(5, down_rows, down_full)
            sp.wait_ge(acc_open, 1)
            sp.dma_start(gate_slot[1][1], gate_rows[3]).then_inc(gate_full[1][1], 16)
            sp.wait_ge(more_ready, 1)
            more = sp.value_load(more_i[0:1, 0:1], min_val=0, max_val=MAX_PASS - 1)

            def load_up(g, h):
                sp.wait_ge(up_done, g - 1)
                for k in range(2):
                    sp.dma_start(up_slot[h][k],
                                 expert_view(up_rows, (g % PAIRS) * 2 + k)).then_inc(up_full[h][k], 16)

            def load_gate(g, h):
                sp.wait_ge(gate_done, g - 1)
                for k in range(2):
                    sp.dma_start(gate_slot[h][k],
                                 expert_view(gate_rows, (g % PAIRS) * 2 + k)).then_inc(gate_full[h][k], 16)

            def load_down(g):
                sp.wait_ge(down_done, g)
                for k in range(2):
                    sp.dma_start(expert_slot[4 + k][:, :],
                                 expert_view(down_rows, (g % PAIRS) * 2 + k)).then_inc(down_full[k], 16)

            ahead = PAIRS - 8
            with sp.Fori(0, more * (PAIRS // 2) + ahead // 2) as i:
                for h in range(2):
                    g = i * 2 + h
                    load_up(g + 2, h)
                    load_gate(g + 2, h)
                    load_down(g + 1)
            g = more * PAIRS + ahead
            last = more * PAIRS + PAIRS - 1
            load_up(g + 2, 0)
            load_down(g + 1)
            for k in (2, 3):
                load_gate(g + k, k % 2)
                load_up(g + k + 1, (k + 1) % 2)
                load_down(g + k)
            load_gate(g + 4, 0)
            load_down(g + 4)
            for k in range(5, PAIRS - 2 - ahead):
                load_up(g + k, k % 2)
                load_gate(g + k, k % 2)
                load_down(g + k)
            load_up(last - 1, 0)
            load_gate(last - 1, 0)
            load_gate(last, 1)
            load_down(last - 1)
            load_up(last, 1)
            sp.wait_ge(up_done, last)
            for n in range(2):
                for k in range(2):
                    sp.dma_start(last_w[k][:, :, n * 512:(n + 1) * 512],
                                 down_rows[E - 2 + k].rearrange("p (j d) -> p j d", j=KF)
                                 [:, :, n * 512:(n + 1) * 512]).then_inc(last_full[n][k], 16)
            out_rows = out.rearrange("b (t p) d -> t (b p) d", p=P)
            for t in range(TT):
                sp.wait_ge(out_ready, t + 1)
                sp.dma_start(out_rows[t], xn[:, t, :]).then_inc(out_written, 16)
            sp.wait_ge(out_written, 16 * TT)

        @block.gpsimd
        def _(pool):
            steps = [0]

            def step(ins):
                ins.then_inc(pool_step, 1)
                steps[0] += 1
                pool.wait_ge(pool_step, steps[0])

            step(nc.gpsimd.memset(ones[:, :], 1.0))
            step(nc.gpsimd.memset(fold[:, :], 1.0 / 32))
            step(nc.gpsimd.memset(ident[:, :], 0.0))
            step(nc.gpsimd.affine_select(out=ident[:, :], in_=ident[:, :], compare_op=ALU.not_equal, fill=1.0, base=0,
                                    pattern=[[-1, P]], channel_multiplier=1))
            step(nc.gpsimd.memset(before[:, :], 1.0))
            step(nc.gpsimd.affine_select(out=before[:, :], in_=before[:, :], compare_op=ALU.is_gt, fill=0.0, base=0,
                                    pattern=[[1, P]], channel_multiplier=-1))
            for i in range(HALF):
                f = float(np.float32(ROPE_BASE ** (-2.0 * i / DH)))
                step(nc.gpsimd.memset(inv_freq[:, i:i + 1], f))
            step(nc.gpsimd.iota(dist, pattern=[[1, S]], base=0, channel_multiplier=-1,
                           allow_small_or_imprecise_dtypes=True))
            step(nc.gpsimd.iota(slot_ids[:, :], pattern=[[1, (MAX_PASS + 1) * SLOTS]], base=0, channel_multiplier=0,
                           allow_small_or_imprecise_dtypes=True))
            step(nc.gpsimd.iota(rev[:, :], pattern=[[-1, EG]], base=EG, channel_multiplier=0,
                           allow_small_or_imprecise_dtypes=True))
            step(nc.gpsimd.memset(eps_col[:, 0:1], EPS))
            step(nc.gpsimd.memset(eps_col[:, 1:2], GN_EPS))
            step(nc.gpsimd.memset(conv_groups[:, :], 0.0))
            step(nc.gpsimd.memset(conv_groups[0:64, 0:64], 1.0 / 64))
            step(nc.gpsimd.memset(conv_groups[64:128, 64:128], 1.0 / 64))
            for j in range(KC - 1):
                step(nc.gpsimd.memset(u_pad[:, :, j:j + 1], 0.0))
            pool.sem_inc(consts, 1)
            for i, tile in enumerate((gate_mix, gate_ffn, final_g)):
                pool.wait_ge(wide_in, 16 * 3)
                if i:
                    pool.wait_ge(wide_ready, i)
                nc.gpsimd.partition_broadcast(tile[:, :], wide_rows[:, i * D:(i + 1) * D], P).then_inc(wide_ready, 1)
            pool.wait_ge(fold_read, 12)
            nc.gpsimd.tensor_tensor(gate_ffn[:, :], gate_fold[:, :], gate_ffn[:, :], ALU.add).then_inc(gate_ready, 1)

        @block.tensor
        def _(pe):
            mm = nc.tensor.matmul

            def unit(key):
                n = unit_index[key]
                pe.wait_ge(ring_full[n % RING], 16 * (n // RING + 1))
                return ring[n % RING][:, :].rearrange("p (j f) -> p j f", j=KD)

            def wait_hT(which, j):
                pe.wait_ge(hT_act if j % 4 < 2 else hT_dve, which * KD // 2 + j // 4 * 2 + 2)

            def turn_x(t, count, banks_of):
                pe.wait_ge(xn_ready, count)
                for j in range(KD):
                    dst = banks_of[:, j * S + t * P:j * S + (t + 1) * P]
                    last = nc.tensor.transpose(dst, xn[:, t, j::KD], ident[:, :])
                return last

            pe.wait_ge(consts, 1)
            pe.wait_ge(c_ready, 1)

            def ada(u, dst=ps_part):
                w = unit(("ada", u))
                if u >= 1:
                    pe.wait_ge(part_read, u)
                for j in range(KD):
                    q = j % 4
                    last = mm(dst[32 * q:32 * q + 32, :], c_wide[:, j, :], w[:, j, :],
                              start=(j < 4), stop=(j >= 4))
                last.then_inc(part_done, 1)

            def fold_unit(u, rows=ps_fold):
                pe.wait_ge(part_read, u + 1)
                if u:
                    pe.wait_ge(fold_read, u)
                vec, half = u // 2, u % 2
                weights = ones if u in BY_DVE else fold
                if vec in (2, 5):
                    mm(rows, weights[:, :], part[:, u % 2, :], start=True, stop=True).then_inc(fold_done, 1)
                else:
                    lo = 64 * half
                    for j in range(KD):
                        last = mm(ps_fold[lo:lo + 64, j:j + 1], part[:, u % 2, j::KD], weights[:, 0:1],
                                  start=True, stop=True)
                    last.then_inc(fold_done, 1)

            def win_tokens(name, dst, between=None):
                w = unit(("win", column_sets.index(name)))
                for t in range(TT):
                    for j in range(KD):
                        if name == used[0] and t == 0:
                            wait_hT(0, j)
                        last = mm(dst[:, t * U:(t + 1) * U], hT[:, j, t * P:(t + 1) * P], w[:, j, :],
                                  start=(j == 0), stop=(j == KD - 1))
                    if between and t == 0:
                        between()
                last.then_inc(win_done, 1)

            def win_channels(name, dst):
                w = unit(("win", column_sets.index(name)))
                for m in range(CT4):
                    for j in range(KD):
                        last = mm(dst[:, m * S:(m + 1) * S], w[:, j, m * P:(m + 1) * P], hT[:, j, :],
                                  start=(j == 0), stop=(j == KD - 1))
                last.then_inc(win_done, 1)

            def turn(src, done):
                for m in range(CT4):
                    for t in range(TT):
                        last = nc.tensor.transpose(ps_s[:, m * S + t * P:m * S + (t + 1) * P],
                                                   src[:, t, m * P:(m + 1) * P], ident[:, :])
                last.then_inc(done, 1)

            def scores(h):
                lo = 64 * (h % 2)
                if h >= 2:
                    pe.wait_ge(weighted_ready, h - 1)
                dst = ps_s[:, (h % 2) * 512:(h % 2) * 512 + S + P]
                mm(dst[:, 0:S], kT[lo:lo + 64, h // 2, 0:P], qT[lo:lo + 64, h // 2, :], start=True, stop=True)
                mm(dst[:, S:S + P], kT[lo:lo + 64, h // 2, P:S], qT[lo:lo + 64, h // 2, P:S],
                   start=True, stop=True).then_inc(scores_done, 1)

            def apply_v(h):
                w = weighted[h]
                y0 = ps_q[:, h * DH:(h + 1) * DH]
                y1 = ps_q[:, RW + h * DH:RW + (h + 1) * DH]
                mm(y0, w[:, 0:P], v_sb[:, 0, h * DH:(h + 1) * DH], start=True, stop=True)
                mm(y1, w[:, P:S], v_sb[:, 0, h * DH:(h + 1) * DH], start=True, stop=False)
                mm(y1, w[:, S:S + P], v_sb[:, 1, h * DH:(h + 1) * DH], start=False, stop=True).then_inc(pv_done, 1)

            def conv_means():
                pe.wait_ge(convsq_ready, 1)
                pe.wait_ge(weighted_ready, H)
                for i in range(2):
                    last = mm(ps_s[:, i * 512:(i + 1) * 512], conv_groups[:, :],
                              b_sb[:, 2 * i:2 * i + 2, :].rearrange("p m s -> p (m s)"), start=True, stop=True)
                last.then_inc(convms_done, 1)

            for u in range(4):
                ada(u)
                fold_unit(u)
                if 1 <= u <= TT:
                    last = turn_x(u - 1, u, banks(2, 4))
                    if u == TT:
                        last.then_inc(xT_done, 1)
            win_tokens("q", ps_p)
            pe.wait_ge(rows_in, 16 * 4)
            nc.tensor.transpose(ps_s[:, 0:(KC + 3) * CT4], small_rows,
                                ident[0:(KC + 3) * CT4, 0:(KC + 3) * CT4]).then_inc(smallT_done, 1)
            win_tokens("k", ps_q)
            fold_unit(4)
            pe.wait_ge(q_ready, 2 * TT)
            win_channels("h", ps_p)
            fold_unit(5)
            pe.wait_ge(smallT_read, 1)
            turn(q_rot, qT_done)
            pe.wait_ge(k_ready, 2 * TT)
            win_channels("c", ps_q)
            fold_unit(6)
            pe.wait_ge(qT_ready, 1)
            turn(k_rot, kT_done)
            pe.wait_ge(h_read, 1)
            win_channels("b", ps_p)
            fold_unit(7)
            pe.wait_ge(kT_ready, 1)
            scores(0)
            scores(1)
            pe.wait_ge(u_ready, 1)
            win_tokens("g", ps_q, between=lambda: (scores(2), scores(3)))
            scores(4)
            scores(5)
            fold_unit(8)
            scores(6)
            scores(7)
            pe.wait_ge(b_ready, 1)
            win_tokens("v", ps_p, between=conv_means)
            fold_unit(9)
            pe.wait_ge(g_read, 1)
            pe.wait_ge(v_ready, 1)
            for h in range(H):
                apply_v(h)
            wo = [unit(("wout", 0)), unit(("wout", 1))]
            pe.wait_ge(yT_conv, 1)
            dst = [ps_s, ps_q]

            def project(n, t, k):
                return mm(dst[n][:, t * U:(t + 1) * U], yT(k)[:, t * P:(t + 1) * P], wo[n][:, k, :],
                          start=(k == CT4), stop=(k == CT4 - 1))

            def project_conv(n, t):
                for k in range(CT4, KD):
                    project(n, t, k)

            def project_ret(n):
                for t in range(TT):
                    for k in range(CT4):
                        last = project(n, t, k)
                    last.then_inc(wout_done, 1)

            project_conv(0, 0)
            project_conv(0, 1)
            pe.wait_ge(yret_ready, 1)
            pe.wait_ge(fold_read, 10)
            for m in range(CT4):
                for t in range(TT):
                    last = nc.tensor.transpose(ps_yT[:, m * S + t * P:m * S + (t + 1) * P],
                                               q_rot[:, t, m * P:(m + 1) * P], ident[:, :])
            last.then_inc(yretT_done, 1)
            project_conv(1, 0)
            pe.wait_ge(yT_ret, CT4)
            project_ret(0)
            project_conv(1, 1)
            project_ret(1)

            pe.wait_ge(x1_ready, 1)
            ada(10, ps_s[:, 0:U])
            turn_x(0, TT + 1, banks(0, 4))
            turn_x(1, TT + 2, banks(0, 4)).then_inc(xT_done, 1)
            fold_unit(10, ps_s[:, 0:U])
            pe.wait_ge(router_in, 16 * 4)
            for j in range(KD):
                wait_hT(1, j)
                last = mm(ps_q[0:G + E, 0:S], router_w[:, j, :], hT[:, j, :], start=(j == 0), stop=(j == KD - 1))
            last.then_inc(logitsT_done, 1)
            pe.wait_ge(logitsT_ready, 1)
            for t in range(TT):
                last = nc.tensor.transpose(ps_q[:, 512 + t * (G + E):512 + (t + 1) * (G + E)],
                                           lgT[:, t * P:(t + 1) * P], ident[0:G + E, 0:G + E])
            last.then_inc(logits_done, 1)
            pe.wait_ge(x1_ready, 2)
            ada(11, ps_s[:, U:2 * U])
            for t in range(TT):
                for n in range(2):
                    b = 2 * t + n
                    last = mm(ps_acc[:, b * 512:(b + 1) * 512], ident[:, :], x_sb[:, t, n * 512:(n + 1) * 512],
                              start=True, stop=False, skip_group_check=True)
            last.then_inc(acc_open, 1)
            fold_unit(11, ps_s[:, U:2 * U])
            pe.wait_ge(mask_ready, 1)
            rank = ps_s[:, 0:TT * E]
            count = ps_s[:, 512:512 + E]
            mm(rank[:, 0:E], before[:, :], msk[:, 0, :], start=True, stop=True)
            mm(rank[:, E:2 * E], ones[:, :], msk[:, 0, :], start=True, stop=False)
            mm(rank[:, E:2 * E], before[:, :], msk[:, 1, :], start=False, stop=True)
            pe.wait_ge(fold_read, 12)
            mm(count, ones[:, :], msk[:, 0, :], start=True, stop=False)
            mm(count, ones[:, :], msk[:, 1, :], start=False, stop=True).then_inc(rank_done, 1)

            def gather(g1):
                pe.wait_ge(pick_ready, g1)
                for j in range(KD):
                    for t in range(TT):
                        last = mm(ps_xy[:, j * 2 * SLOTS:(j + 1) * 2 * SLOTS], xn[:, t, j::KD], pick[:, t, :],
                                  start=(t == 0), stop=(t == TT - 1))
                last.then_inc(gather_done, 1)

            def scatter(t, n, last_pair=False):
                b = 2 * t + n
                return mm(ps_acc[:, b * 512:(b + 1) * 512], placeT[:, t * P:(t + 1) * P],
                          y_sb[:, n * 512:(n + 1) * 512], start=False, stop=last_pair, skip_group_check=True)

            def expert_in(dst, w):
                for j in range(KD):
                    for k in range(2):
                        last = mm(dst[64 * k:64 * k + 64, :], xgT[:, j, 64 * k:64 * k + 64], w[k][:, j, :],
                                  start=(j == 0), stop=(j == KD - 1))
                return last

            def expert_out(n, w):
                for j in range(KF):
                    for k in range(2):
                        last = mm(ps_xy[64 * k:64 * k + 64, n * 512:(n + 1) * 512], hidT[:, j, 64 * k:64 * k + 64],
                                  w[k][:, j, n * 512:(n + 1) * 512], start=(j == 0), stop=(j == KF - 1))
                return last

            def up(g, h, landed):
                pe.wait_ge(xg_lo, g + 1)
                pe.wait_ge(xg_hi, g + 1)
                pe.wait_ge(placeT_ready, g + 1)
                for k in range(2):
                    pe.wait_ge(up_full[h][k], landed)
                expert_in(ps_up, up_w[h]).then_inc(up_done, 1)

            def gate(g, h, landed):
                pe.wait_ge(xg_lo, g + 1)
                pe.wait_ge(xg_hi, g + 1)
                pe.wait_ge(hidT_ready, g + 1)
                for k in range(2):
                    pe.wait_ge(gate_full[h][k], landed)
                expert_in(ps_gate, gate_w[h]).then_inc(gate_done, 1)

            def add_before(g):
                pe.wait_ge(placeT_ready, g + 1)
                pe.wait_ge(y_ready, g + 1)
                for t in range(TT):
                    for n in range(2):
                        scatter(t, n)

            def turn_hidden(g):
                pe.wait_ge(hid_ready, g + 1)
                for j in range(KF):
                    nc.tensor.transpose(ps_gate[:, j * P:(j + 1) * P], hid[:, j::KF], ident[:, :])
                pe.wait_ge(place_ready, g + 1)
                for t in range(TT):
                    last = nc.tensor.transpose(ps_up[:, t * P:(t + 1) * P], place[:, t, :], ident[:, :])
                last.then_inc(turned, 1)

            def down(g):
                pe.wait_ge(hidT_ready, g + 2)
                pe.wait_ge(xg_lo, g + 2)
                pe.wait_ge(xg_hi, g + 2)
                for k in range(2):
                    pe.wait_ge(down_full[k], g * 16 + 16)
                expert_out(0, down_w)
                expert_out(1, down_w).then_inc(down_done, 1)

            def pair(g, h, landed):
                up(g, h, landed)
                gate(g, h, landed)
                add_before(g)
                gather(g + 2)
                turn_hidden(g)

            gather(1)
            pe.wait_ge(more_ready, 1)
            more = pe.value_load(more_i[0:1, 0:1], min_val=0, max_val=MAX_PASS - 1)
            with pe.Fori(0, more * (PAIRS // 2) + PAIRS // 2 - 1) as i:
                for h in range(2):
                    pair(i * 2 + h, h, i * 16 + 16)
                    down(i * 2 + h)
            landed = more * (PAIRS * 8) + PAIRS * 8
            g = more * PAIRS + PAIRS - 1
            pair(g - 1, 0, landed)
            gate(g, 1, landed)
            down(g - 1)
            add_before(g)
            up(g, 1, landed)
            turn_hidden(g)
            pe.wait_ge(hidT_ready, g + 2)
            for n in range(2):
                for k in range(2):
                    pe.wait_ge(last_full[n][k], 16)
                expert_out(n, last_w).then_inc(down_done, 1)
            pe.wait_ge(placeT_ready, g + 2)
            for n in range(2):
                pe.wait_ge(y_ready, g + 2 + n)
                for t in range(TT):
                    scatter(t, n, True).then_inc(acc_done, 1)

        @block.scalar
        def _(act):
            steps = [0]

            def step(ins):
                ins.then_inc(act_step, 1)
                steps[0] += 1
                act.wait_ge(act_step, steps[0])

            act.wait_ge(c_in, 16)
            nc.scalar.activation(cvec[:, 1, :], cvec[:, 0, :], ACT.Exp, scale=-1.0).then_inc(c_exp, 1)
            act.dma_start(pos_i[:, :], positions.rearrange("b (t p) -> (b p) t", p=P),
                          allow_slow_non_contiguous=True).then_inc(pos_in, 16)
            for i, rows in enumerate((beta_ret, beta_conv, conv_b)):
                act.dma_start(small_rows[i * CT4:(i + 1) * CT4, :],
                              rows.rearrange("l (t p) -> (l t) p", p=P)).then_inc(rows_in, 16)
            act.dma_start(small_rows[3 * CT4:(3 + KC) * CT4, :],
                          conv_w.rearrange("l k (t p) -> (l k t) p", p=P)).then_inc(rows_in, 16)
            for i, row in enumerate((ada_b[:, 2 * D:3 * D], ada_b[:, 5 * D:6 * D],
                                     norm_final_g.rearrange("(a d) -> a d", a=1))):
                act.dma_start(wide_rows[:, i * D:(i + 1) * D], row).then_inc(wide_in, 16)
            act.dma_start(router_w[:, :, 0:G],
                          router_group_w.rearrange("l (p j) g -> (l p) j g", p=P)).then_inc(router_in, 16)
            act.dma_start(router_w[:, :, G:G + E],
                          router_expert_w.rearrange("l (p j) g -> (l p) j g", p=P)).then_inc(router_in, 16)
            act.dma_start(router_b[0:G, :], router_group_b.rearrange("l g -> g l")).then_inc(router_in, 16)
            act.dma_start(router_b[G:G + E, :], router_expert_b.rearrange("l g -> g l")).then_inc(router_in, 16)

            def root(which, t, part):
                nc.scalar.activation(rms[:, which, t:t + 1], mean_sq[:, which, t, part:part + 1], ACT.Sqrt,
                                     bias=eps_col[:, 0:1] if part == 0 else mean_sq[:, which, t, 2:3]
                                     ).then_inc(root_ready, 1)

            n_sq = [0]

            def square(which, t, part, cols):
                src = acc[:, t, cols] if which == 2 else x_sb[:, t, cols]
                nc.scalar.activation(xn[:, t, cols], src, ACT.Square, scale=D ** -0.5,
                                     accum_out=mean_sq[:, which, t, part:part + 1]).then_inc(squares, 1)
                n_sq[0] += 1

            def half_norm(which, t, n):
                square(which, t, n, slice(n * U, (n + 1) * U))
                act.wait_ge(squares, n_sq[0])
                if n == 0:
                    nc.scalar.activation(mean_sq[:, which, t, 2:3], mean_sq[:, which, t, 0:1], ACT.Identity,
                                         bias=eps_col[:, 0:1]).then_inc(squares, 1)
                    n_sq[0] += 1
                else:
                    root(which, t, 1)

            act.wait_ge(x_in, 16)
            for t in range(TT):
                square(0, t, 0, slice(0, D))
            act.wait_ge(squares, n_sq[0])
            act.wait_ge(consts, 1)
            for t in range(TT):
                root(0, t, 0)

            def part_copy(u, src=ps_part):
                act.wait_ge(*unit_used(unit_index[("ada", u)]))
                if u >= 2:
                    act.wait_ge(fold_done, u - 1)
                nc.scalar.copy(part[:, u % 2, :], src).then_inc(part_read, 1)

            def hT_by_act(which, src):
                for j in (0, 1, 4, 5):
                    nc.scalar.activation(hT[:, j, :], src[:, j * S:(j + 1) * S], ACT.Identity,
                                         scale=scale_a[:, which, j:j + 1],
                                         bias=modcol[:, 2 * which, j:j + 1]).then_inc(hT_act, 1)

            def channels(ap):
                return ap.rearrange("p (m s) -> p m s", m=CT4)

            def tokens(ap):
                return ap.rearrange("p (t n) -> p t n", t=TT)

            for u in range(4):
                part_copy(u)
            act.wait_ge(xT_done, 1)
            act.wait_ge(scales_ready, 1)
            hT_by_act(0, banks(2, 4))
            act.wait_ge(trig_arg_ready, 1)
            nc.scalar.activation(trig, trig_arg[:, 3], ACT.Sin).then_inc(trig_ready, 1)
            act.wait_ge(decay_ready, 1)
            for h in range(H):
                lg_h = float(np.log1p(-np.exp2(np.float32(-5.0 - h))).astype(np.float32))
                nc.scalar.activation(decay[:, h, :], dist, ACT.Exp, scale=lg_h).then_inc(decay_masked, 1)
            act.wait_ge(win_done, win_turn["h"])
            nc.scalar.copy(conv_y[:, :, :], channels(ps_p)).then_inc(h_read, 1)
            act.wait_ge(qT_done, 1)
            nc.scalar.copy(qT[:, :, :], channels(ps_s)).then_inc(qT_ready, 1)
            act.wait_ge(kT_done, 1)
            nc.scalar.copy(kT, channels(ps_s)).then_inc(kT_ready, 1)
            act.wait_ge(win_done, win_turn["b"])
            nc.scalar.copy(b_sb, channels(ps_p)).then_inc(b_ready, 1)
            act.wait_ge(convy_ready, 1)
            nc.scalar.activation(b_sb, conv_y[:, :, :], ACT.Square).then_inc(convsq_ready, 1)
            act.wait_ge(win_done, win_turn["g"])
            nc.scalar.activation(g_silu, tokens(ps_q), ACT.Exp, scale=-1.0).then_inc(g_exp, 1)
            nc.scalar.copy(g_raw, tokens(ps_q)).then_inc(g_read, 1)
            act.wait_ge(convms_done, 1)
            nc.scalar.activation(b_sb, channels(ps_s), ACT.Sqrt, bias=eps_col[:, 0:1]).then_inc(convroot_ready, 1)
            act.wait_ge(win_done, win_turn["v"])
            nc.scalar.copy(v_sb, tokens(ps_p)).then_inc(v_ready, 1)
            act.wait_ge(centered, 1)
            nc.scalar.activation(k_rot, q_rot, ACT.Square).then_inc(centered_sq, 1)
            act.wait_ge(gnvar_ready, 1)
            nc.scalar.activation(groups[:, 2, :], groups[:, 1, :], ACT.Sqrt, bias=eps_col[:, 1:2],
                                 scale=1.0 / DH).then_inc(gnroot_ready, 1)
            act.wait_ge(yretT_done, 1)
            for m in range(CT4):
                nc.scalar.activation(yT(m), ps_yT[:, m * S:(m + 1) * S], ACT.Copy,
                                     scale=small_cols[:, m:m + 1]).then_inc(yT_ret, 1)
            for n in range(2):
                for t in range(TT):
                    act.wait_ge(x1_ready, TT * n + t + 1)
                    half_norm(1, t, n)
            part_copy(10, ps_s[:, 0:U])
            act.wait_ge(xT_done, 2)
            hT_by_act(1, banks(0, 4))
            act.wait_ge(fold_done, 11)
            nc.scalar.copy(gate_fold[:, 0:U], ps_s[:, 0:U]).then_inc(fold_read, 1)
            act.wait_ge(logitsT_done, 1)
            act.wait_ge(router_in, 16 * 4)
            nc.scalar.activation(lgT[:, :], ps_q[0:G + E, 0:S], ACT.Identity,
                                 bias=router_b[:, 0:1]).then_inc(logitsT_ready, 1)
            act.wait_ge(group_shift, 1)
            nc.scalar.activation(rt[:, 1, :, 0:G], rt[:, 0, :, 0:G], ACT.Exp).then_inc(group_exp, 1)
            part_copy(11, ps_s[:, U:2 * U])
            act.wait_ge(expert_shift, 1)
            nc.scalar.activation(rt[:, 5, :, :], rt[:, 4, :, :], ACT.Exp).then_inc(expert_exp, 1)
            act.wait_ge(fold_done, 12)
            nc.scalar.copy(gate_fold[:, U:D], ps_s[:, U:2 * U]).then_inc(fold_read, 1)

            def gathered_lo(g1):
                act.wait_ge(gather_done, g1)
                for j in range(KD // 2):
                    last = nc.scalar.activation(xgT[:, j, :], ps_xy[:, j * P:(j + 1) * P], ACT.Identity,
                                                scale=scale_a[:, 1, j:j + 1], bias=modcol[:, 2, j:j + 1])
                last.then_inc(xg_lo, 1)

            def pair(g, last_pair=False):
                act.wait_ge(gate_done, g + 1)
                nc.scalar.activation(ea, ps_gate, ACT.Exp, scale=-1.0).then_inc(ea_ready, 1)
                if last_pair:
                    nc.scalar.activation(rms[:, 0, 0:1], eps_col[:, 0:1], ACT.Sqrt)
                if not last_pair:
                    gathered_lo(g + 2)
                act.wait_ge(turned, g + 1)
                nc.scalar.copy(placeT, ps_up[:, 0:TT * P]).then_inc(placeT_ready, 1)

            gathered_lo(1)
            act.wait_ge(more_ready, 1)
            more = act.value_load(more_i[0:1, 0:1], min_val=0, max_val=MAX_PASS - 1)
            with act.Fori(0, more * (PAIRS // 2) + PAIRS // 2 - 1) as i:
                for h in range(2):
                    pair(i * 2 + h)
            pair(more * PAIRS + PAIRS - 2)
            pair(more * PAIRS + PAIRS - 1, last_pair=True)
            for n in range(2):
                for t in range(TT):
                    act.wait_ge(acc_done, n * TT + t + 1)
                    half_norm(2, t, n)

        @block.vector
        def _(dve):
            v = nc.vector
            steps = [0]

            def step(ins):
                ins.then_inc(dve_step, 1)
                steps[0] += 1
                dve.wait_ge(dve_step, steps[0])

            tt, ts, stt = v.tensor_tensor, v.tensor_scalar, v.scalar_tensor_tensor

            dve.wait_ge(c_exp, 1)
            step(ts(cvec[:, 2, :], cvec[:, 1, :], 1.0, None, ALU.add))
            step(v.reciprocal(cvec[:, 3, :], cvec[:, 2, :]))
            step(tt(cvec[:, 2, :], cvec[:, 3, :], cvec[:, 0, :], ALU.mult))
            v.tensor_copy(c_wide, cvec[:, 2, :].unsqueeze(2).broadcast_to([P, KD, 32])).then_inc(c_ready, 1)

            def norm_rows(which, t, count):
                dve.wait_ge(root_ready, count)
                step(v.reciprocal(inv_rms[:, which, t:t + 1], rms[:, which, t:t + 1]))
                ts(xn[:, t, :], x_sb[:, t, :], inv_rms[:, which, t:t + 1], None, ALU.mult).then_inc(xn_ready, 1)

            for t in range(TT):
                norm_rows(0, t, TT)
            dve.wait_ge(consts, 1)

            def fold_read_out(u):
                vec, half = u // 2, u % 2
                dve.wait_ge(fold_done, u + 1)
                if vec in (2, 5):
                    dst = (gate_mix if vec == 2 else gate_ffn)[:, half * U:(half + 1) * U]
                    tt(dst, ps_fold, dst, ALU.add).then_inc(fold_read, 1)
                else:
                    lo = 64 * half
                    tt(modcol[lo:lo + 64, {0: 0, 1: 1, 3: 2, 4: 3}[vec], :], ps_fold[lo:lo + 64, 0:KD],
                       mod_bias[lo:lo + 64, vec, :], ALU.add).then_inc(fold_read, 1)

            def ada_sums(u):
                n = unit_index[("ada", u)]
                w = ring[n % RING][:, :].rearrange("p (j f) -> p j f", j=KD)
                dst = part[:, u % 2, :]
                dve.wait_ge(ring_full[n % RING], 16 * (n // RING + 1))
                dve.wait_ge(fold_done, u - 1)
                step(ts(dst, w[:, 0, :], cvec[:, 2, 0:1], None, ALU.mult))
                for j in range(1, KD - 1):
                    step(stt(dst, w[:, j, :], cvec[:, 2, j:j + 1], dst, ALU.mult, ALU.add))
                stt(dst, w[:, KD - 1, :], cvec[:, 2, KD - 1:KD], dst, ALU.mult, ALU.add).then_inc(part_read, 1)

            def scales(which, count):
                dve.wait_ge(fold_read, count)
                stt(scale_a[:, which, :], modcol[:, 2 * which + 1, :], 1.0, norm_g[:, which, :],
                    ALU.add, ALU.mult).then_inc(scales_ready, 1)

            def hT_by_dve(which, src):
                for j in (2, 3, 6, 7):
                    ts(hT[:, j, :], src[:, j * S:(j + 1) * S], scale_a[:, which, j:j + 1],
                       modcol[:, 2 * which, j:j + 1], ALU.mult, ALU.add).then_inc(hT_dve, 1)

            dve.wait_ge(mod_in, 16 * 3)
            for u in range(4):
                fold_read_out(u)
            scales(0, 4)
            dve.wait_ge(scales_ready, 1)
            dve.wait_ge(xT_done, 1)
            hT_by_dve(0, banks(2, 4))
            dve.wait_ge(pos_in, 16)
            step(v.tensor_copy(pos_f, pos_i[:, :]))
            angle, turns, red, arg = (trig_arg[:, i] for i in range(4))
            for t in range(TT):
                ts(angle[:, 1, t, :], inv_freq, pos_f[:, t:t + 1], None, ALU.mult).then_inc(dve_step, 1)
                steps[0] += 1
            dve.wait_ge(dve_step, steps[0])
            for i, quarter in ((0, 0.25), (1, 0.0)):
                step(ts(turns[:, i], angle[:, 1], 1.0 / TWO_PI, quarter, ALU.mult, ALU.add))
                step(ts(red[:, i], turns[:, i], ROUND, None, ALU.add))
                step(ts(turns[:, i], red[:, i], -ROUND, None, ALU.add))
                step(stt(red[:, i], turns[:, i], -TWO_PI_HI, angle[:, 1], ALU.mult, ALU.add))
                step(stt(arg[:, i], turns[:, i], -TWO_PI_MID, red[:, i], ALU.mult, ALU.add))
                step(stt(red[:, i], turns[:, i], -TWO_PI_LO, arg[:, i], ALU.mult, ALU.add))
                step(ts(turns[:, i], red[:, i], (1 - i) * np.pi / 2, -PI_BELOW, ALU.add, ALU.max))
                last = ts(arg[:, i], turns[:, i], PI_BELOW, None, ALU.min)
                if i == 0:
                    step(last)
            last.then_inc(trig_arg_ready, 1)
            stt(dist, dist, -1.0, dist, ALU.mult, ALU.max).then_inc(decay_ready, 1)
            dve.wait_ge(trig_ready, 1)

            def rotate(src, dst, ready):
                for t in range(TT):
                    s3 = src[:, t * RW:(t + 1) * RW].rearrange("p (a f) -> p a f", f=HALF)
                    cos = trig[:, 0, t, :].unsqueeze(1).broadcast_to([P, 2 * H, HALF])
                    sin = trig[:, 1, t, :].unsqueeze(1).broadcast_to([P, 2 * H, HALF])
                    if t:
                        dve.wait_ge(ready, 2 * t)
                    tt(tmp_c.rearrange("p (a f) -> p a f", f=HALF), s3, cos, ALU.mult).then_inc(dve_step, 1)
                    step_n()
                    step(tt(tmp_s.rearrange("p (a f) -> p a f", f=HALF), s3, sin, ALU.mult))
                    c4 = tmp_c.rearrange("p (h a f) -> p h a f", a=2, f=HALF)
                    s4 = tmp_s.rearrange("p (h a f) -> p h a f", a=2, f=HALF)
                    d4 = dst[:, t].rearrange("p (h a f) -> p h a f", a=2, f=HALF)
                    tt(d4[:, :, 0, :], c4[:, :, 0, :], s4[:, :, 1, :], ALU.subtract).then_inc(ready, 1)
                    tt(d4[:, :, 1, :], c4[:, :, 1, :], s4[:, :, 0, :], ALU.add).then_inc(ready, 1)

            def step_n():
                steps[0] += 1

            def weigh(h):
                dve.wait_ge(scores_done, h + 1)
                src = ps_s[:, (h % 2) * 512:(h % 2) * 512 + S + P]
                stt(weighted[h][:, 0:S], src[:, 0:S], DH ** -0.5, decay[:, h, :],
                    ALU.mult, ALU.mult).then_inc(dve_step, 1)
                step_n()
                stt(weighted[h][:, S:S + P], src[:, S:S + P], DH ** -0.5, decay[:, h, 0:P],
                    ALU.mult, ALU.mult).then_inc(weighted_ready, 1)

            taps = small_cols[:, 3 * CT4:(3 + KC) * CT4].rearrange("p (k m) -> p k m", k=KC)

            def conv(m):
                step(ts(conv_y[:, m, :], u_pad[:, m, KC - 1:KC - 1 + S], taps[:, KC - 1, m:m + 1],
                        small_cols[:, 2 * CT4 + m:2 * CT4 + m + 1], ALU.mult, ALU.add))
                for k in range(KC - 1):
                    step(stt(conv_y[:, m, :], u_pad[:, m, k:k + S], taps[:, k, m:m + 1], conv_y[:, m, :],
                             ALU.mult, ALU.add))

            dve.wait_ge(wide_ready, 3)
            dve.wait_ge(win_done, win_turn["q"])
            rotate(ps_p, q_rot, q_ready)
            dve.wait_ge(q_ready, 2 * TT)
            dve.wait_ge(smallT_done, 1)
            v.tensor_copy(small_cols[:, :], ps_s[:, 0:(KC + 3) * CT4]).then_inc(smallT_read, 1)
            ada_sums(4)
            dve.wait_ge(win_done, win_turn["k"])
            rotate(ps_q, k_rot, k_ready)
            fold_read_out(4)
            ada_sums(5)
            fold_read_out(5)
            dve.wait_ge(decay_masked, H)
            v.memset(decay[64:128, :, 0:64], 0.0).then_inc(dve_step, 1)
            steps[0] += 1
            dve.wait_ge(dve_step, steps[0])
            ada_sums(6)

            dve.wait_ge(smallT_read, 1)
            dve.wait_ge(h_read, 1)
            dve.wait_ge(win_done, win_turn["c"])
            tt(u_pad[:, :, KC - 1:KC - 1 + S], conv_y[:, :, :], ps_q.rearrange("p (m s) -> p m s", m=CT4),
               ALU.mult).then_inc(u_ready, 1)
            fold_read_out(6)
            dve.wait_ge(u_ready, 1)
            for m in range(CT4):
                conv(m)
            ada_sums(7)
            fold_read_out(7)
            weigh(0)
            weigh(1)
            dve.wait_ge(b_ready, 1)
            tt(conv_y[:, :, :], conv_y[:, :, :], b_sb, ALU.mult).then_inc(convy_ready, 1)
            ada_sums(8)
            weigh(2)
            weigh(3)
            ada_sums(9)
            weigh(4)
            weigh(5)
            fold_read_out(8)
            weigh(6)
            weigh(7)
            dve.wait_ge(g_exp, 1)
            step(ts(g_silu, g_silu, 1.0, None, ALU.add))
            step(v.reciprocal(g_silu, g_silu))
            dve.wait_ge(g_read, 1)
            tt(g_silu, g_silu, g_raw, ALU.mult).then_inc(g_ready, 1)
            dve.wait_ge(convroot_ready, 1)
            step(v.reciprocal(b_sb, b_sb))
            for m in range(CT4):
                last = stt(qT[:, m, :], conv_y[:, m, :], small_cols[:, CT4 + m:CT4 + m + 1], b_sb[:, m, :],
                           ALU.mult, ALU.mult)
            last.then_inc(yT_conv, 1)
            fold_read_out(9)

            dve.wait_ge(pv_done, H)
            y3 = ps_q.rearrange("p (a f) -> p a f", f=DH)
            q3 = q_rot.rearrange("p t (h f) -> p (t h) f", f=DH)
            k3 = k_rot.rearrange("p t (h f) -> p (t h) f", f=DH)
            g3 = g_silu.rearrange("p t (h f) -> p (t h) f", f=DH)

            def per_head(ap):
                return ap.unsqueeze(2).broadcast_to([P, TT * H, DH])

            step(v.tensor_reduce(groups[:, 0, :], y3, AX.X, ALU.add))
            step(ts(groups[:, 1, :], groups[:, 0, :], 1.0 / DH, None, ALU.mult))
            tt(q3, y3, per_head(groups[:, 1, :]), ALU.subtract).then_inc(centered, 1)
            dve.wait_ge(centered_sq, 1)
            v.tensor_reduce(groups[:, 1, :], k3, AX.X, ALU.add).then_inc(gnvar_ready, 1)
            dve.wait_ge(g_ready, 1)
            step(tt(g3, g3, q3, ALU.mult))
            dve.wait_ge(gnroot_ready, 1)
            step(v.reciprocal(groups[:, 0, :], groups[:, 2, :]))
            tt(q3, g3, per_head(groups[:, 0, :]), ALU.mult).then_inc(yret_ready, 1)
            scales(1, 10)
            dve.wait_ge(scales_ready, 2)
            v.memset(placeT, 0.0).then_inc(zero_ready, 1)
            v.memset(y_sb, 0.0).then_inc(zero_ready, 1)
            dve.wait_ge(zero_ready, 2)
            dve.sem_inc(y_ready, 1)

            def residual(t, n, src, gate):
                cols = slice(n * U, (n + 1) * U)
                step(tt(xn[:, t, cols], src, gate[:, cols], ALU.mult))
                tt(x_sb[:, t, cols], x_sb[:, t, cols], xn[:, t, cols], ALU.add).then_inc(x1_ready, 1)

            for n, src in ((0, ps_s), (1, ps_q)):
                for t in range(TT):
                    dve.wait_ge(wout_done, n * TT + t + 1)
                    residual(t, n, src[:, t * U:(t + 1) * U], gate_mix)
                    if n == 1:
                        norm_rows(1, t, TT + t + 1)
            dve.wait_ge(xT_done, 2)
            hT_by_dve(1, banks(0, 4))

            dve.wait_ge(logits_done, 1)

            def wide(ap, n):
                return ap.broadcast_to([P, TT, n])

            lg = ps_q[:, 512:512 + TT * (G + E)].rearrange("p (t n) -> p t n", t=TT)
            glg, elg = lg[:, :, 0:G], lg[:, :, G:G + E].rearrange("p t (g e) -> p t g e", g=G)
            col = lambda i: rt[:, 15, :, i:i + 1]
            step(v.tensor_reduce(col(0), glg, AX.X, ALU.max))
            tt(rt[:, 0, :, 0:G], glg, wide(col(0), G), ALU.subtract).then_inc(group_shift, 1)
            dve.wait_ge(group_exp, 1)

            def first_max(probs, n, top, work, onehot):
                step(v.tensor_reduce(top, probs, AX.X, ALU.max))
                step(tt(work, probs, wide(top, n), ALU.is_equal))
                step(tt(work, work, rev[:, EG - n:EG].unsqueeze(1).broadcast_to([P, TT, n]), ALU.mult))
                step(v.tensor_reduce(col(7), work, AX.X, ALU.max))
                step(tt(onehot, work, wide(col(7), n), ALU.is_equal))

            gp = rt[:, 1, :, 0:G]
            group_hot = rt[:, 3, :, 0:G]
            first_max(gp, G, col(1), rt[:, 2, :, 0:G], group_hot)
            step(v.tensor_reduce(col(2), gp, AX.X, ALU.add))
            ohe4 = ohe.rearrange("p t (g e) -> p t g e", g=G)
            step(tt(ohe4, elg, group_hot.unsqueeze(3).broadcast_to([P, TT, G, EG]), ALU.mult))
            step(v.tensor_reduce(rt[:, 6, :, :], ohe.rearrange("p t (g e) -> p t e g", g=G), AX.X, ALU.add))
            step(v.tensor_reduce(col(0), rt[:, 6, :, :], AX.X, ALU.max))
            tt(rt[:, 4, :, :], rt[:, 6, :, :], wide(col(0), EG), ALU.subtract).then_inc(expert_shift, 1)
            dve.wait_ge(expert_exp, 1)
            first_max(rt[:, 5, :, :], EG, col(3), rt[:, 7, :, :], rt[:, 8, :, :])
            step(stt(rt[:, 9, :, :], rt[:, 8, :, :], -4.0, rt[:, 5, :, :], ALU.mult, ALU.add))
            first_max(rt[:, 9, :, :], EG, col(4), rt[:, 7, :, :], rt[:, 10, :, :])
            step(tt(within8[:, 1], rt[:, 8, :, :], rt[:, 10, :, :], ALU.add))
            gh4 = group_hot.unsqueeze(3).broadcast_to([P, TT, G, EG])

            def spread(i):
                return within8[:, i].unsqueeze(2).broadcast_to([P, TT, G, EG])

            tt(msk.rearrange("p t (g e) -> p t g e", g=G), spread(1), gh4, ALU.mult).then_inc(mask_ready, 1)
            dve.wait_ge(mask_ready, 1)
            dve.wait_ge(rank_done, 1)
            step(stt(ohe[:, :, :], ps_s[:, 0:TT * E].rearrange("p (t e) -> p t e", t=TT), 1.0, msk[:, :, :],
                     ALU.add, ALU.mult))
            step(ts(posm[:, :, :], ohe[:, :, :], -1.0, None, ALU.add))

            def pick_pair(e, ids):
                for k in range(2):
                    for t in range(TT):
                        last = ts(pick[:, t, k * SLOTS:(k + 1) * SLOTS], slot_ids[:, ids],
                                  posm[:, t, bass.ds(e + k, 1)], None, ALU.is_equal)
                last.then_inc(pick_ready, 1)

            def gathered_hi(g1):
                dve.wait_ge(gather_done, g1)
                for j in range(KD // 2, KD):
                    last = ts(xgT[:, j, :], ps_xy[:, j * P:(j + 1) * P], scale_a[:, 1, j:j + 1],
                              modcol[:, 2, j:j + 1], ALU.mult, ALU.add)
                last.then_inc(xg_hi, 1)

            pick_pair(0, slice(0, SLOTS))
            step(v.tensor_reduce(cnt[:, 0:1], ps_s[:, 512:512 + E], AX.X, ALU.max))
            step(ts(rt[0:1, 13, 0, 0:MAX_PASS - 1], slot_ids[0:1, SLOTS:MAX_PASS * SLOTS:SLOTS], cnt[0:1, 0:1], None,
                    ALU.is_lt))
            step(v.tensor_reduce(cnt[0:1, 1:2], rt[0:1, 13, 0, 0:MAX_PASS - 1], AX.X, ALU.add))
            v.tensor_copy(more_i[0:1, 0:1], cnt[0:1, 1:2]).then_inc(more_ready, 1)
            step(tt(col(5), col(3), col(4), ALU.add))
            step(tt(col(6), col(5), col(2), ALU.mult))
            step(v.reciprocal(col(5), col(6)))
            step(tt(col(6), col(5), col(1), ALU.mult))
            step(tt(col(0), col(3), col(6), ALU.mult))
            step(tt(col(5), col(4), col(6), ALU.mult))
            step(tt(rt[:, 11, :, :], rt[:, 8, :, :], wide(col(0), EG), ALU.mult))
            step(tt(rt[:, 12, :, :], rt[:, 10, :, :], wide(col(5), EG), ALU.mult))
            step(tt(within8[:, 0], rt[:, 11, :, :], rt[:, 12, :, :], ALU.add))
            step(tt(combine[:, :, :].rearrange("p t (g e) -> p t g e", g=G), spread(0), gh4, ALU.mult))
            dve.sem_inc(hidT_ready, 1)
            dve.sem_inc(placeT_ready, 1)
            dve.wait_ge(more_ready, 1)
            more = dve.value_load(more_i[0:1, 0:1], min_val=0, max_val=MAX_PASS - 1)
            dve.wait_ge(gate_ready, 1)
            gathered_hi(1)
            base = steps[0]

            def pair(g, last_pair=False):
                if not last_pair:
                    pick_pair(((g + 1) % PAIRS) * 2, bass.ds(((g + 1) // PAIRS) * SLOTS, SLOTS))
                e = (g % PAIRS) * 2
                ids = bass.ds((g // PAIRS) * SLOTS, SLOTS)
                for k in range(2):
                    for t in range(TT):
                        last = ts(place[:, t, k * SLOTS:(k + 1) * SLOTS], slot_ids[:, ids],
                                  posm[:, t, bass.ds(e + k, 1)], combine[:, t, bass.ds(e + k, 1)],
                                  ALU.is_equal, ALU.mult)
                last.then_inc(place_ready, 1)
                dve.wait_ge(ea_ready, g + 1)
                ts(hid, ea, 1.0, None, ALU.add).then_inc(dve_step, 1)
                dve.wait_ge(dve_step, g * 3 + (base + 1))
                v.reciprocal(ea, hid).then_inc(dve_step, 1)
                dve.wait_ge(dve_step, g * 3 + (base + 2))
                tt(hid, ea, ps_gate, ALU.mult).then_inc(dve_step, 1)
                dve.wait_ge(dve_step, g * 3 + (base + 3))
                dve.wait_ge(up_done, g + 1)
                tt(hid, hid, ps_up, ALU.mult).then_inc(hid_ready, 1)
                if not last_pair:
                    gathered_hi(g + 2)
                dve.wait_ge(turned, g + 1)
                v.tensor_copy(hidT, ps_gate.rearrange("p (j s) -> p j s", j=KF)).then_inc(hidT_ready, 1)
                for n, cols in enumerate((slice(0, U), slice(U, D)) if last_pair else (slice(0, D),)):
                    dve.wait_ge(down_done, g + n + 1)
                    tt(y_sb[:, cols], ps_xy[:, cols], gate_ffn[:, cols], ALU.mult).then_inc(y_ready, 1)

            with dve.Fori(0, more * (PAIRS // 2) + PAIRS // 2 - 1) as i:
                for h in range(2):
                    pair(i * 2 + h)
            pair(more * PAIRS + PAIRS - 2)
            pair(more * PAIRS + PAIRS - 1, last_pair=True)

            for t in range(TT):
                dve.wait_ge(root_ready, 2 * TT + t + 1)
                v.reciprocal(inv_rms[:, 2, t:t + 1], rms[:, 2, t:t + 1]).then_inc(last_step, 1)
                dve.wait_ge(last_step, t + 1)
                stt(xn[:, t, :], acc[:, t, :], inv_rms[:, 2, t:t + 1], final_g[:, :],
                    ALU.mult, ALU.mult).then_inc(out_ready, 1)


_INS = ["x", "c", "positions", "ada_w", "ada_b", "norm_mix_g", "norm_ffn_g", "w_in", "conv_w", "conv_b", "beta_ret",
        "beta_conv", "w_out", "router_group_w", "router_group_b", "router_expert_w", "router_expert_b",
        "expert_w_gate", "expert_w_up", "expert_w_down", "norm_final_g"]


def kernel(**inputs):
    import numpy as _np
    import concourse.bacc as _bacc
    from concourse import mybir as _mybir
    from concourse.bass_utils import run_bass_kernel_spmd as _run

    nc = _bacc.Bacc("TRN2", target_bir_lowering=False, num_devices=1)
    arrays, args = {}, []
    for name in _INS:
        a = _np.ascontiguousarray(inputs[name])
        arrays[f"in_{name}"] = a
        args.append(nc.dram_tensor(f"in_{name}", a.shape, _mybir.dt.from_np(a.dtype), kind="ExternalInput").ap())
    out = nc.dram_tensor("out_0", inputs["x"].shape, F32, kind="ExternalOutput").ap()
    hybrid_retention_moe_layer(nc, *args, out)
    r = _run(nc, [arrays], core_ids=[0])
    return r.results[0]["out_0"]
```

```python
from contextlib import ExitStack

import concourse.bass as bass
import numpy as np
from concourse import mybir

F32 = mybir.dt.float32
I32 = mybir.dt.int32
ALU = mybir.AluOpType
ACT = mybir.ActivationFunctionType
AX = mybir.AxisListType

P = 128
EPS = 1e-6
GN_EPS = 1e-5
ROPE_BASE = 10000.0
TWO_PI = 2.0 * np.pi
PI_BELOW = 3.1415925
TWO_PI_HI = 6.28125
TWO_PI_MID = float(np.float32(0.0019350051879882812))
TWO_PI_LO = float(np.float32(TWO_PI - TWO_PI_HI - TWO_PI_MID))
ROUND = 12582912.0
SLOTS = 64
RING = 6


def hybrid_retention_moe_layer(nc, x, c, positions, ada_w, ada_b, norm_mix_g, norm_ffn_g, w_in, conv_w, conv_b,
                               beta_ret, beta_conv, w_out, router_group_w, router_group_b, router_expert_w,
                               router_expert_b, expert_w_gate, expert_w_up, expert_w_down, norm_final_g, out):
    _, S, D = x.shape
    TT = S // P
    KD = D // P
    CHUNK = 64
    RW = D // 2
    H = 8
    DH = RW // H
    HALF = DH // 2
    CT4 = RW // P
    KC = conv_w.shape[1]
    G = router_group_w.shape[2]
    EG = expert_w_gate.shape[2]
    E = G * EG
    F = expert_w_gate.shape[4]
    KF = F // P
    PAIRS = E // 2
    U = 512
    MAX_PASS = S // SLOTS
    assert S == 256 and D == 1024 and RW == 512 and F == 512 and DH == CHUNK == 64

    gate_rows = expert_w_gate.rearrange("l g e (p j) f -> (l g e) p (j f)", p=P)
    up_rows = expert_w_up.rearrange("l g e (p j) f -> (l g e) p (j f)", p=P)
    down_rows = expert_w_down.rearrange("l g e (p j) f -> (l g e) p (j f)", p=P)
    ada_rows = ada_w.rearrange("l (p j) n -> (l p) j n", p=P)
    win_rows = w_in.rearrange("l (p j) n -> (l p) j n", p=P)
    wout_rows = w_out.rearrange("l (t p) n -> (l p) t n", p=P)

    units = [("ada", u) for u in range(4)]
    column_sets = ("q", "k", "v", "g", "b", "c", "h")
    used = ("q", "k", "h", "c", "b", "g", "v")
    for i, name in enumerate(used):
        units += [("win", column_sets.index(name))] + ([("ada", 4 + i)] if i < 6 else [])
    win_turn = {name: i + 1 for i, name in enumerate(used)}
    units += [("wout", 0), ("wout", 1), ("ada", 10), ("ada", 11)]
    BY_DVE = range(4, 12)
    unit_index = {key: n for n, key in enumerate(units)}
    NU = len(units)

    with ExitStack() as ctx:
        def sb(name, shape, dt=F32):
            return ctx.enter_context(nc.sbuf_tensor(name, shape, dt))

        def sem(name):
            return ctx.enter_context(nc.semaphore(name))

        ring = [sb(f"ring{i}", [P, KD * U]) for i in range(RING)]
        expert_slot = [ring[(NU + k) % RING] for k in range(6)]
        last_w = [expert_slot[k][:, :].rearrange("p (j d) -> p j d", j=KF) for k in (0, 1)]
        down_w = [expert_slot[k][:, :].rearrange("p (j d) -> p j d", j=KF) for k in (4, 5)]

        xn = sb("xn", [P, TT, D])

        late_gate = sb("late_gate", [P, 2, KD * F])
        conv_y = late_gate[:, 0, 0:CT4 * S].rearrange("p (m s) -> p m s", m=CT4)
        qT = late_gate[:, 0, CT4 * S:2 * CT4 * S].rearrange("p (m s) -> p m s", m=CT4)
        gate_mix = late_gate[:, 0, 2 * CT4 * S:2 * CT4 * S + D]
        spare = 2 * CT4 * S + D
        small_rows = late_gate[0:(KC + 3) * CT4, 0, spare:spare + P]
        groups = late_gate[:, 0, spare + P:spare + P + 3 * TT * H].rearrange("p (i a) -> p i a", i=3)
        conv_groups = late_gate[:, 0, spare + 2 * P:spare + 3 * P]
        hT = late_gate[:, 1, 0:KD * S].rearrange("p (j s) -> p j s", j=KD)
        x_sb = late_gate[:, 1, KD * S:KD * S + TT * D].rearrange("p (t d) -> p t d", t=TT)
        yT_ret_half = hT[:, 0:CT4, :]
        gate_ffn = sb("gate_ffn", [P, D])
        final_g = sb("final_g", [P, D])
        ident = sb("ident", [P, P])
        before = sb("before", [P, P])
        ones = sb("ones", [P, P])
        fold = sb("fold", [P, P])
        slot_ids = sb("slot_ids", [P, (MAX_PASS + 1) * SLOTS])
        rev = sb("rev", [P, EG])
        eps_col = sb("eps_col", [P, 2])
        router_w = sb("router_w", [P, KD, G + E])
        router_b = sb("router_b", [G + E, 1])
        mod_bias = sb("mod_bias", [P, 6, KD])
        norm_g = sb("norm_g", [P, 2, KD])
        modcol = sb("modcol", [P, 4, KD])
        scale_a = sb("scale_a", [P, 2, KD])
        small_cols = sb("small_cols", [P, (KC + 3) * CT4])
        mean_sq = sb("mean_sq", [P, 3, TT, 3])
        rms = sb("rms", [P, 3, TT])
        inv_rms = sb("inv_rms", [P, 3, TT])
        part = sb("part", [P, 2, U])
        posm = sb("posm", [P, TT, E])
        combine = sb("combine", [P, TT, E])
        more_i = sb("more_i", [1, 1], I32)

        x_flat = xn[:, :, :].rearrange("p t d -> p (t d)")
        ARENA = 12640
        arena = sb("arena", [P, ARENA])
        taken = [0]

        def front(shape):
            n = int(np.prod(shape))
            ap = arena[:, taken[0]:taken[0] + n]
            taken[0] += n
            assert taken[0] <= ARENA
            if len(shape) == 1:
                return ap
            names = "abcd"[:len(shape)]
            return ap.rearrange("p (%s) -> p %s" % (" ".join(names), " ".join(names)),
                                **{k: v for k, v in zip(names, shape)})

        decay = front([H, S])
        kT = front([CT4, S])
        g_raw = front([TT, RW])
        tmp_c, tmp_s = g_raw[:, 0], g_raw[:, 1]
        assert taken[0] == KD * F
        b_sb = front([CT4, S])
        v_sb = front([TT, RW])
        u_pad = front([CT4, S + KC - 1])
        trig = front([2, TT, HALF])
        trig_arg = front([4, 2, TT, HALF])
        inv_freq = front([HALF])
        pos_f = front([TT])
        dist = front([S])
        taken[0] = 2 * KD * F
        wide_rows = arena[0:1, taken[0]:taken[0] + 3 * D]
        q_rot = front([TT, RW])
        k_rot = front([TT, RW])
        g_silu = front([TT, RW])
        scored = front([3, S + P])
        weighted = [x_flat[:, h * (S + P):(h + 1) * (S + P)] for h in range(5)] + [scored[:, h] for h in range(3)]
        cvec = sb("cvec", [P, 4, KD])
        c_wide_flat = sb("c_wide", [P, KD * 32])
        c_wide = c_wide_flat[:, :].rearrange("p (j c) -> p j c", j=KD)
        lgT = sb("lgT", [G + E, S])
        lg_sb = sb("lg_sb", [P, TT, G + E])
        shift_col = sb("shift_col", [G + E, 1])
        shift_rows = sb("shift_rows", [P, G + E])
        shift_diag = sb("shift_diag", [G + E, G + E])
        rt = sb("rt", [P, 16, TT, EG])
        within8 = sb("within8", [P, 2, TT, EG])
        msk = sb("msk", [P, TT, E])
        ohe = sb("ohe", [P, TT, E])
        cnt = sb("cnt", [P, 4])
        pos_i = sb("pos_i", [P, TT], I32)

        late_up = arena[:, 0:2 * KD * F].rearrange("p (k n) -> p k n", k=2)
        up_slot = [[expert_slot[k][:, :] for k in (0, 1)], [late_up[:, k, :] for k in (0, 1)]]
        gate_slot = [[expert_slot[k][:, :] for k in (2, 3)], [late_gate[:, k, :] for k in (0, 1)]]
        gate_w = [[ap.rearrange("p (j f) -> p j f", j=KD) for ap in pair] for pair in gate_slot]
        up_w = [[ap.rearrange("p (j f) -> p j f", j=KD) for ap in pair] for pair in up_slot]
        taken[0] = 2 * KD * F
        xgT = front([KD, 2 * SLOTS])
        pick = front([TT, 2 * SLOTS])
        place = front([TT, 2 * SLOTS])
        placeT = front([TT * P])
        gate_fold = arena[:, taken[0]:taken[0] + D]
        hid = front([F])
        ea = front([F])
        hidT = front([KF, 2 * SLOTS])
        y_sb = front([D])

        ps = ctx.enter_context(nc.psum_tensor("ps", [P, 8, 512], F32))

        def banks(a, n):
            return ps[:, a:a + n, :].rearrange("p b c -> p (b c)")

        ps_part = banks(0, 1)
        ps_fold = banks(1, 1)

        def partials(u):
            return ps_part if u % 2 == 0 else banks(6, 1)

        ps_p = banks(2, 2)
        ps_q = banks(4, 2)
        ps_s = banks(6, 2)
        ps_yT = banks(0, 2)
        ps_acc = banks(0, 4)
        acc = ps_acc.rearrange("p (t d) -> p t d", t=TT)
        ps_xy = banks(4, 2)
        ps_gate = banks(6, 1)
        ps_up = banks(7, 1)

        ring_full = [sem(f"ring_full{i}") for i in range(RING)]
        up_full = [[[sem(f"up_full{h}{k}{b}") for b in range(2)] for k in range(2)] for h in range(2)]
        gate_full = [[sem(f"gate_full{h}{k}") for k in range(2)] for h in range(2)]
        down_full = [sem("down_full0"), sem("down_full1")]
        last_full = [[sem(f"last_full{n}{k}") for k in range(2)] for n in range(2)]
        gate_done = sem("gate_done")
        up_done = sem("up_done")
        down_done = sem("down_done")
        x_in = sem("x_in")
        c_in = sem("c_in")
        pos_in = sem("pos_in")
        mod_in = sem("mod_in")
        rows_in = sem("rows_in")
        router_in = sem("router_in")
        wide_in = sem("wide_in")
        wide_ready = sem("wide_ready")
        h_read = sem("h_read")
        g_read = sem("g_read")
        logitsT_done = sem("logitsT_done")
        logitsT_ready = sem("logitsT_ready")
        last_step = sem("last_step")
        out_written = sem("out_written")
        consts = sem("consts")
        act_step = sem("act_step")
        dve_step = sem("dve_step")
        pool_step = sem("pool_step")
        c_exp = sem("c_exp")
        c_ready = sem("c_ready")
        squares = sem("squares")
        rms_ready = sem("rms_ready")
        root_ready = sem("root_ready")
        xn_ready = sem("xn_ready")
        trig_arg_ready = sem("trig_arg_ready")
        trig_ready = sem("trig_ready")
        decay_ready = sem("decay_ready")
        decay_masked = sem("decay_masked")
        xT_done = sem("xT_done")
        part_done = sem("part_done")
        part_read = sem("part_read")
        fold_done = sem("fold_done")
        fold_read = sem("fold_read")
        smallT_done = sem("smallT_done")
        smallT_read = sem("smallT_read")
        scales_ready = sem("scales_ready")
        hT_act = sem("hT_act")
        hT_dve = sem("hT_dve")
        win_done = sem("win_done")
        q_ready = sem("q_ready")
        k_ready = sem("k_ready")
        v_first = sem("v_first")
        v_ready = sem("v_ready")
        g_exp = sem("g_exp")
        g_ready = sem("g_ready")
        b_ready = sem("b_ready")
        c_read = sem("c_read")
        u_ready = sem("u_ready")
        qT_done = sem("qT_done")
        qT_ready = sem("qT_ready")
        kT_done = sem("kT_done")
        kT_ready = sem("kT_ready")
        scores_done = sem("scores_done")
        weighted_ready = sem("weighted_ready")
        pv_done = sem("pv_done")
        convy_ready = sem("convy_ready")
        convsq_ready = sem("convsq_ready")
        convms_done = sem("convms_done")
        convroot_ready = sem("convroot_ready")
        yT_conv = sem("yT_conv")
        centered = sem("centered")
        centered_sq = sem("centered_sq")
        gnvar_ready = sem("gnvar_ready")
        gnroot_ready = sem("gnroot_ready")
        yret_ready = sem("yret_ready")
        yretT_done = sem("yretT_done")
        yT_ret = sem("yT_ret")
        wout_done = sem("wout_done")
        x1_ready = sem("x1_ready")
        logits_done = sem("logits_done")
        shift_done = sem("shift_done")
        shift_read = sem("shift_read")
        diag_ready = sem("diag_ready")
        shift_spread = sem("shift_spread")
        shift_ready = sem("shift_ready")
        group_shift = sem("group_shift")
        group_exp = sem("group_exp")
        expert_shift = sem("expert_shift")
        expert_exp = sem("expert_exp")
        mask_ready = sem("mask_ready")
        rank_done = sem("rank_done")
        count_done = sem("count_done")
        more_ready = sem("more_ready")
        pick_ready = sem("pick_ready")
        place_ready = sem("place_ready")
        gather_done = sem("gather_done")
        xg_lo = sem("xg_lo")
        xg_hi = sem("xg_hi")
        ea_ready = sem("ea_ready")
        hid_ready = sem("hid_ready")
        turned = sem("turned")
        hidT_ready = sem("hidT_ready")
        placeT_ready = sem("placeT_ready")
        y_ready = sem("y_ready")
        gate_ready = sem("gate_ready")
        acc_open = sem("acc_open")
        acc_done = sem("acc_done")
        out_ready = sem("out_ready")

        block = ctx.enter_context(nc.Block())

        def expert_view(ap, e):
            return ap[bass.ds(e, 1)].rearrange("e p n -> p (e n)")

        def yT(k):
            return yT_ret_half[:, k, :] if k < CT4 else qT[:, k - CT4, :]

        def unit_used(n):
            kind, u = units[n]
            if kind == "win":
                return win_done, win_turn[column_sets[u]]
            if kind == "wout":
                return wout_done, (u + 1) * TT
            if u in BY_DVE:
                return part_read, u + 1
            return part_done, u + 1

        @block.sync
        def _(sp):
            sp.dma_start(x_sb[:, :, :], x.rearrange("b (t p) d -> (b p) t d", p=P)).then_inc(x_in, 16)
            sp.dma_start(cvec[:, 0, :], c.rearrange("b (p j) -> (b p) j", p=P)).then_inc(c_in, 16)
            sp.dma_start(pos_i[:, :], positions.rearrange("b (t p) -> (b p) t", p=P),
                          allow_slow_non_contiguous=True).then_inc(pos_in, 16)
            sp.dma_start(mod_bias[:, :, :], ada_b.rearrange("l (v p j) -> (l p) v j", v=6, p=P)).then_inc(mod_in, 16)
            sp.dma_start(norm_g[:, 0, :], norm_mix_g.rearrange("l (p j) -> (l p) j", p=P)).then_inc(mod_in, 16)
            sp.dma_start(norm_g[:, 1, :], norm_ffn_g.rearrange("l (p j) -> (l p) j", p=P)).then_inc(mod_in, 16)
            for n, (kind, u) in enumerate(units):
                if n == RING:
                    for i, rows in enumerate((beta_ret, beta_conv, conv_b)):
                        sp.dma_start(small_rows[i * CT4:(i + 1) * CT4, :],
                                      rows.rearrange("l (t p) -> (l t) p", p=P)).then_inc(rows_in, 16)
                    sp.dma_start(small_rows[3 * CT4:(3 + KC) * CT4, :],
                                  conv_w.rearrange("l k (t p) -> (l k t) p", p=P)).then_inc(rows_in, 16)
                    for i, row in enumerate((ada_b[:, 2 * D:3 * D], ada_b[:, 5 * D:6 * D],
                                             norm_final_g.rearrange("(a d) -> a d", a=1))):
                        sp.dma_start(wide_rows[:, i * D:(i + 1) * D], row).then_inc(wide_in, 16)
                    sp.dma_start(router_w[:, :, 0:G],
                                  router_group_w.rearrange("l (p j) g -> (l p) j g", p=P)).then_inc(router_in, 16)
                    sp.dma_start(router_w[:, :, G:G + E],
                                  router_expert_w.rearrange("l (p j) g -> (l p) j g", p=P)).then_inc(router_in, 16)
                    sp.dma_start(router_b[0:G, :], router_group_b.rearrange("l g -> g l")).then_inc(router_in, 16)
                    sp.dma_start(router_b[G:G + E, :], router_expert_b.rearrange("l g -> g l")).then_inc(router_in, 16)
                if n >= RING:
                    sp.wait_ge(*unit_used(n - RING))
                rows = {"ada": ada_rows, "win": win_rows, "wout": wout_rows}[kind]
                sp.dma_start(ring[n % RING][:, :].rearrange("p (j f) -> p j f", j=KD),
                             rows[:, :, u * U:(u + 1) * U]).then_inc(ring_full[n % RING], 16)
            def load_first(k, rows, full):
                sp.wait_ge(*unit_used(NU - RING + k))
                sp.dma_start(expert_slot[k][:, :], rows[k % 2]).then_inc(full[k % 2], 16)

            HALF_W = KD * F // 2

            def half(ap, b):
                return ap[:, b * HALF_W:(b + 1) * HALF_W]

            def load_first_up(k, pair):
                for b in range(2):
                    sp.dma_start(half(up_slot[pair][k], b),
                                 half(up_rows[2 * pair + k], b)).then_inc(up_full[pair][k][b], 16)

            sp.wait_ge(*unit_used(NU - RING))
            load_first_up(0, 0)
            sp.wait_ge(weighted_ready, H)
            sp.wait_ge(g_ready, 1)
            load_first_up(0, 1)
            sp.wait_ge(*unit_used(NU - RING + 1))
            load_first_up(1, 0)
            sp.wait_ge(pv_done, H)
            sp.wait_ge(yT_conv, 1)
            load_first_up(1, 1)
            for k in (4, 2, 5, 3):
                load_first(k, gate_rows if k < 4 else down_rows, gate_full[0] if k < 4 else down_full)
            sp.wait_ge(x1_ready, 2 * TT)
            sp.dma_start(gate_slot[1][0], gate_rows[2]).then_inc(gate_full[1][0], 16)
            sp.wait_ge(acc_open, 1)
            sp.dma_start(gate_slot[1][1], gate_rows[3]).then_inc(gate_full[1][1], 16)
            sp.wait_ge(more_ready, 1)
            more = sp.value_load(more_i[0:1, 0:1], min_val=0, max_val=MAX_PASS - 1)

            def load_up(g, h, halves=(0, 1)):
                for b in halves:
                    sp.wait_ge(up_done, g * 2 - 3 + b)
                    for k in range(2):
                        sp.dma_start(half(up_slot[h][k], b),
                                     half(expert_view(up_rows, (g % PAIRS) * 2 + k), b)).then_inc(up_full[h][k][b], 16)

            def load_gate(g, h):
                sp.wait_ge(gate_done, g - 1)
                for k in range(2):
                    sp.dma_start(gate_slot[h][k],
                                 expert_view(gate_rows, (g % PAIRS) * 2 + k)).then_inc(gate_full[h][k], 16)

            def load_down(g):
                sp.wait_ge(down_done, g)
                for k in range(2):
                    sp.dma_start(expert_slot[4 + k][:, :],
                                 expert_view(down_rows, (g % PAIRS) * 2 + k)).then_inc(down_full[k], 16)

            ahead = PAIRS - 10
            load_up(2, 0, (0,))
            load_gate(2, 0)
            load_up(2, 0, (1,))
            load_down(1)
            load_up(3, 1)
            load_gate(3, 1)
            load_down(2)
            with sp.Fori(0, more * (PAIRS // 2) + ahead // 2 - 1) as i:
                for h in range(2):
                    g = i * 2 + (h + 2)
                    load_up(g + 2, h)
                    load_gate(g + 2, h)
                    load_down(g + 1)
            g = more * PAIRS + ahead
            last = more * PAIRS + PAIRS - 1
            load_up(g + 2, 0)
            load_down(g + 1)
            for k in (2, 3, 4):
                load_gate(g + k, k % 2)
                load_up(g + k + 1, (k + 1) % 2)
                load_down(g + k)
            load_gate(g + 5, 1)
            load_down(g + 5)
            for k in (6, 7):
                load_up(g + k, k % 2)
                load_gate(g + k, k % 2)
                load_down(g + k)
            load_up(last - 1, 0)
            load_gate(last - 1, 0)
            load_gate(last, 1)
            load_down(last - 1)
            load_up(last, 1)
            sp.wait_ge(up_done, last * 2)
            for n in range(2):
                for k in range(2):
                    sp.dma_start(last_w[k][:, :, n * 512:(n + 1) * 512],
                                 down_rows[E - 2 + k].rearrange("p (j d) -> p j d", j=KF)
                                 [:, :, n * 512:(n + 1) * 512]).then_inc(last_full[n][k], 16)
            out_rows = out.rearrange("b (t p) d -> t (b p) d", p=P)
            for t in range(TT):
                sp.wait_ge(out_ready, t + 1)
                sp.dma_start(out_rows[t], xn[:, t, :]).then_inc(out_written, 16)
            sp.wait_ge(out_written, 16 * TT)

        @block.gpsimd
        def _(pool):
            steps = [0]

            def step(ins):
                ins.then_inc(pool_step, 1)
                steps[0] += 1
                pool.wait_ge(pool_step, steps[0])

            step(nc.gpsimd.memset(ones[:, :], 1.0))
            step(nc.gpsimd.memset(fold[:, :], 1.0 / 32))
            step(nc.gpsimd.memset(ident[:, :], 0.0))
            step(nc.gpsimd.affine_select(out=ident[:, :], in_=ident[:, :], compare_op=ALU.not_equal, fill=1.0, base=0,
                                    pattern=[[-1, P]], channel_multiplier=1))
            step(nc.gpsimd.memset(before[:, :], 1.0))
            step(nc.gpsimd.affine_select(out=before[:, :], in_=before[:, :], compare_op=ALU.is_gt, fill=0.0, base=0,
                                    pattern=[[1, P]], channel_multiplier=-1))
            for i in range(HALF):
                f = float(np.float32(ROPE_BASE ** (-2.0 * i / DH)))
                step(nc.gpsimd.memset(inv_freq[:, i:i + 1], f))
            step(nc.gpsimd.iota(dist, pattern=[[1, S]], base=0, channel_multiplier=-1,
                           allow_small_or_imprecise_dtypes=True))
            step(nc.gpsimd.iota(slot_ids[:, :], pattern=[[1, (MAX_PASS + 1) * SLOTS]], base=1, channel_multiplier=0,
                           allow_small_or_imprecise_dtypes=True))
            step(nc.gpsimd.iota(rev[:, :], pattern=[[-1, EG]], base=EG, channel_multiplier=0,
                           allow_small_or_imprecise_dtypes=True))
            step(nc.gpsimd.memset(eps_col[:, 0:1], EPS))
            step(nc.gpsimd.memset(eps_col[:, 1:2], GN_EPS))
            step(nc.gpsimd.memset(conv_groups[:, :], 0.0))
            step(nc.gpsimd.memset(conv_groups[0:64, 0:64], 1.0 / 64))
            step(nc.gpsimd.memset(conv_groups[64:128, 64:128], 1.0 / 64))
            for j in range(KC - 1):
                step(nc.gpsimd.memset(u_pad[:, :, j:j + 1], 0.0))
            pool.sem_inc(consts, 1)
            for i, tile in enumerate((gate_mix, gate_ffn, final_g)):
                pool.wait_ge(wide_in, 16 * 3)
                if i:
                    pool.wait_ge(wide_ready, i)
                nc.gpsimd.partition_broadcast(tile[:, :], wide_rows[:, i * D:(i + 1) * D], P).then_inc(wide_ready, 1)
            pool.wait_ge(fold_read, 12)
            nc.gpsimd.tensor_tensor(gate_ffn[:, :], gate_fold[:, :], gate_ffn[:, :], ALU.add).then_inc(gate_ready, 1)

        @block.tensor
        def _(pe):
            mm = nc.tensor.matmul

            def unit(key):
                n = unit_index[key]
                pe.wait_ge(ring_full[n % RING], 16 * (n // RING + 1))
                return ring[n % RING][:, :].rearrange("p (j f) -> p j f", j=KD)

            def wait_hT(which, j):
                pe.wait_ge(hT_act if j % 4 < 2 else hT_dve, which * KD // 2 + j // 4 * 2 + 2)

            def turn_x(t, count, banks_of):
                pe.wait_ge(xn_ready, count)
                for j in range(KD):
                    dst = banks_of[:, j * S + t * P:j * S + (t + 1) * P]
                    last = nc.tensor.transpose(dst, xn[:, t, j::KD], ident[:, :])
                return last

            pe.wait_ge(consts, 1)
            pe.wait_ge(c_ready, 1)

            def ada(u, dst=ps_part):
                w = unit(("ada", u))
                if u >= 2:
                    pe.wait_ge(part_read, u - 1)
                for j in range(KD):
                    q = j % 4
                    last = mm(dst[32 * q:32 * q + 32, :], c_wide[:, j, :], w[:, j, :],
                              start=(j < 4), stop=(j >= 4))
                last.then_inc(part_done, 1)

            def fold_unit(u, rows=ps_fold):
                pe.wait_ge(part_read, u + 1)
                if u:
                    pe.wait_ge(fold_read, u)
                vec, half = u // 2, u % 2
                weights = ones if u in BY_DVE else fold
                if vec in (2, 5):
                    mm(rows, weights[:, :], part[:, u % 2, :], start=True, stop=True).then_inc(fold_done, 1)
                else:
                    lo = 64 * half
                    for j in range(KD):
                        last = mm(ps_fold[lo:lo + 64, j:j + 1], part[:, u % 2, j::KD], weights[:, 0:1],
                                  start=True, stop=True)
                    last.then_inc(fold_done, 1)

            def win_tokens(name, dst, between=None):
                w = unit(("win", column_sets.index(name)))
                for t in range(TT):
                    for j in range(KD):
                        if name == used[0] and t == 0:
                            wait_hT(0, j)
                        last = mm(dst[:, t * U:(t + 1) * U], hT[:, j, t * P:(t + 1) * P], w[:, j, :],
                                  start=(j == 0), stop=(j == KD - 1))
                    if t == 0:
                        if name == "v":
                            last.then_inc(v_first, 1)
                        if between:
                            between()
                last.then_inc(win_done, 1)

            def win_channels(name, dst):
                w = unit(("win", column_sets.index(name)))
                for m in range(CT4):
                    for j in range(KD):
                        last = mm(dst[:, m * S:(m + 1) * S], w[:, j, m * P:(m + 1) * P], hT[:, j, :],
                                  start=(j == 0), stop=(j == KD - 1))
                last.then_inc(win_done, 1)

            def turn(src, done):
                for m in range(CT4):
                    for t in range(TT):
                        last = nc.tensor.transpose(ps_s[:, m * S + t * P:m * S + (t + 1) * P],
                                                   src[:, t, m * P:(m + 1) * P], ident[:, :])
                last.then_inc(done, 1)

            def scores(h):
                lo = 64 * (h % 2)
                if h >= 2:
                    pe.wait_ge(weighted_ready, h - 1)
                dst = ps_s[:, (h % 2) * 512:(h % 2) * 512 + S + P]
                mm(dst[:, 0:S], kT[lo:lo + 64, h // 2, 0:P], qT[lo:lo + 64, h // 2, :], start=True, stop=True)
                mm(dst[:, S:S + P], kT[lo:lo + 64, h // 2, P:S], qT[lo:lo + 64, h // 2, P:S],
                   start=True, stop=True).then_inc(scores_done, 1)

            def apply_v(h):
                w = weighted[h]
                y0 = ps_q[:, h * DH:(h + 1) * DH]
                y1 = ps_q[:, RW + h * DH:RW + (h + 1) * DH]
                mm(y0, w[:, 0:P], v_sb[:, 0, h * DH:(h + 1) * DH], start=True, stop=True)
                mm(y1, w[:, P:S], v_sb[:, 0, h * DH:(h + 1) * DH], start=True, stop=False)
                mm(y1, w[:, S:S + P], v_sb[:, 1, h * DH:(h + 1) * DH], start=False, stop=True).then_inc(pv_done, 1)

            def conv_means():
                pe.wait_ge(convsq_ready, 1)
                pe.wait_ge(weighted_ready, H)
                for i in range(2):
                    last = mm(ps_s[:, i * 512:(i + 1) * 512], conv_groups[:, :],
                              b_sb[:, 2 * i:2 * i + 2, :].rearrange("p m s -> p (m s)"), start=True, stop=True)
                last.then_inc(convms_done, 1)

            ada(0)
            for u in range(1, 4):
                ada(u, partials(u))
                fold_unit(u - 1)
                if u >= 2:
                    last = turn_x(u - 2, TT, banks(2, 4))
            last.then_inc(xT_done, 1)
            fold_unit(3)
            win_tokens("q", ps_p)
            pe.wait_ge(rows_in, 16 * 4)
            nc.tensor.transpose(ps_s[:, 0:(KC + 3) * CT4], small_rows,
                                ident[0:(KC + 3) * CT4, 0:(KC + 3) * CT4]).then_inc(smallT_done, 1)
            win_tokens("k", ps_q)
            fold_unit(4)
            pe.wait_ge(q_ready, 2 * TT)
            win_channels("h", ps_p)
            fold_unit(5)
            pe.wait_ge(smallT_read, 1)
            turn(q_rot, qT_done)
            pe.wait_ge(k_ready, 2 * TT)
            win_channels("c", ps_q)
            fold_unit(6)
            pe.wait_ge(qT_ready, 1)
            turn(k_rot, kT_done)
            pe.wait_ge(h_read, 1)
            win_channels("b", ps_p)
            fold_unit(7)
            pe.wait_ge(kT_ready, 1)
            scores(0)
            scores(1)
            pe.wait_ge(u_ready, 1)
            win_tokens("g", ps_q, between=lambda: (scores(2), scores(3)))
            scores(4)
            scores(5)
            fold_unit(8)
            scores(6)
            scores(7)
            pe.wait_ge(b_ready, 1)
            win_tokens("v", ps_p, between=conv_means)
            fold_unit(9)
            pe.wait_ge(g_read, 1)
            pe.wait_ge(v_ready, 2)
            for h in range(H):
                apply_v(h)
            wo = [unit(("wout", 0)), unit(("wout", 1))]
            pe.wait_ge(yT_conv, 1)
            dst = [ps_s, ps_q]

            def project(n, t, k):
                return mm(dst[n][:, t * U:(t + 1) * U], yT(k)[:, t * P:(t + 1) * P], wo[n][:, k, :],
                          start=(k == CT4), stop=(k == CT4 - 1))

            def project_conv(n, t):
                for k in range(CT4, KD):
                    project(n, t, k)

            def project_ret(n):
                for t in range(TT):
                    for k in range(CT4):
                        last = project(n, t, k)
                    last.then_inc(wout_done, 1)

            project_conv(0, 0)
            project_conv(0, 1)
            pe.wait_ge(centered, 1)
            project_conv(1, 0)
            pe.wait_ge(yret_ready, 1)
            pe.wait_ge(fold_read, 10)
            for m in range(CT4):
                for t in range(TT):
                    last = nc.tensor.transpose(ps_yT[:, m * S + t * P:m * S + (t + 1) * P],
                                               q_rot[:, t, m * P:(m + 1) * P], ident[:, :])
            last.then_inc(yretT_done, 1)
            project_conv(1, 1)
            pe.wait_ge(yT_ret, CT4)
            project_ret(0)
            project_ret(1)

            def turn_x1(t):
                pe.wait_ge(x1_ready, TT + t + 1)
                for j in range(KD):
                    last = nc.tensor.transpose(ps_acc[:, j * S + t * P:j * S + (t + 1) * P],
                                               x_sb[:, t, j::KD], ident[:, :])
                return last

            turn_x1(0)
            pe.wait_ge(scales_ready, 2)
            pe.wait_ge(router_in, 16 * 4)
            for j in range(KD):
                last = mm(ps_s[0:G + E, U:U + 1], router_w[:, j, :], modcol[:, 2, j:j + 1],
                          start=(j == 0), stop=(j == KD - 1))
            last.then_inc(shift_done, 1)
            turn_x1(1).then_inc(xT_done, 1)
            fold_unit(10, ps_s[:, 0:U])
            pe.wait_ge(diag_ready, 1)
            mm(ps_q[:, U:U + G + E], ones[0:G + E, :], shift_diag[:, :], start=True, stop=True).then_inc(shift_spread, 1)
            for j in range(KD):
                wait_hT(1, j)
                last = mm(ps_q[0:G + E, 0:S], router_w[:, j, :], hT[:, j, :], start=(j == 0), stop=(j == KD - 1))
            last.then_inc(logitsT_done, 1)
            pe.wait_ge(shift_ready, 1)
            pe.wait_ge(logitsT_ready, 1)
            for t in range(TT):
                last = nc.tensor.transpose(ps_q[:, 512 + t * (G + E):512 + (t + 1) * (G + E)],
                                           lgT[:, t * P:(t + 1) * P], ident[0:G + E, 0:G + E])
            last.then_inc(logits_done, 1)
            pe.wait_ge(shift_read, 1)
            fold_unit(11, ps_s[:, U:2 * U])
            for t in range(TT):
                if t:
                    pe.wait_ge(expert_shift, 1)
                for n in range(2):
                    b = 2 * t + n
                    last = mm(ps_acc[:, b * 512:(b + 1) * 512], ident[:, :], x_sb[:, t, n * 512:(n + 1) * 512],
                              start=True, stop=False, skip_group_check=True)
            last.then_inc(acc_open, 1)
            pe.wait_ge(mask_ready, 1)
            rank = ps_s[:, 0:TT * E]
            count = ps_s[:, 512:512 + E]
            mm(rank[:, 0:E], before[:, :], msk[:, 0, :], start=True, stop=True)
            mm(rank[:, E:2 * E], ones[:, :], msk[:, 0, :], start=True, stop=False)
            mm(rank[:, E:2 * E], before[:, :], msk[:, 1, :], start=False, stop=True).then_inc(rank_done, 1)
            pe.wait_ge(fold_read, 12)
            mm(count, ones[:, :], msk[:, 0, :], start=True, stop=False)
            mm(count, ones[:, :], msk[:, 1, :], start=False, stop=True).then_inc(count_done, 1)

            def gather(g1):
                pe.wait_ge(pick_ready, g1)
                pe.wait_ge(xn_ready, 2 * TT)
                for j in range(KD):
                    for t in range(TT):
                        last = mm(ps_xy[:, j * 2 * SLOTS:(j + 1) * 2 * SLOTS], xn[:, t, j::KD], pick[:, t, :],
                                  start=(t == 0), stop=(t == TT - 1))
                    if j % (KD // 2) == KD // 2 - 1:
                        last.then_inc(gather_done, 1)

            def scatter(t, n, last_pair=False):
                b = 2 * t + n
                return mm(ps_acc[:, b * 512:(b + 1) * 512], placeT[:, t * P:(t + 1) * P],
                          y_sb[:, n * 512:(n + 1) * 512], start=False, stop=last_pair, skip_group_check=True)

            def expert_in(dst, w, blocks):
                for j in blocks:
                    for k in range(2):
                        last = mm(dst[64 * k:64 * k + 64, :], xgT[:, j, 64 * k:64 * k + 64], w[k][:, j, :],
                                  start=(j == 0), stop=(j == KD - 1))
                return last

            def expert_out(n, w):
                for j in range(KF):
                    for k in range(2):
                        last = mm(ps_xy[64 * k:64 * k + 64, n * 512:(n + 1) * 512], hidT[:, j, 64 * k:64 * k + 64],
                                  w[k][:, j, n * 512:(n + 1) * 512], start=(j == 0), stop=(j == KF - 1))
                return last

            def up(g, h, landed, halves=(0, 1)):
                if 0 in halves:
                    pe.wait_ge(placeT_ready, g + 1)
                for b in halves:
                    pe.wait_ge((xg_lo, xg_hi)[b], g + 1)
                    for k in range(2):
                        pe.wait_ge(up_full[h][k][b], landed)
                    expert_in(ps_up, up_w[h], range(b * KD // 2, (b + 1) * KD // 2)).then_inc(up_done, 1)

            def gate(g, h, landed):
                pe.wait_ge(hidT_ready, g + 1)
                for k in range(2):
                    pe.wait_ge(gate_full[h][k], landed)
                pe.wait_ge(xg_lo, g + 1)
                pe.wait_ge(xg_hi, g + 1)
                expert_in(ps_gate, gate_w[h], range(KD)).then_inc(gate_done, 1)

            def add_before(g):
                pe.wait_ge(placeT_ready, g + 1)
                pe.wait_ge(y_ready, g)
                for t in range(TT):
                    for n in range(2):
                        scatter(t, n)

            def turn_hidden(g):
                pe.wait_ge(hid_ready, g + 1)
                for j in range(KF):
                    nc.tensor.transpose(ps_gate[:, j * P:(j + 1) * P], hid[:, j::KF], ident[:, :])
                pe.wait_ge(place_ready, g + 1)
                for t in range(TT):
                    last = nc.tensor.transpose(ps_up[:, t * P:(t + 1) * P], place[:, t, :], ident[:, :])
                last.then_inc(turned, 1)

            def down(g):
                pe.wait_ge(hidT_ready, g + 2)
                pe.wait_ge(xg_lo, g + 2)
                pe.wait_ge(xg_hi, g + 2)
                for k in range(2):
                    pe.wait_ge(down_full[k], g * 16 + 16)
                expert_out(0, down_w)
                expert_out(1, down_w).then_inc(down_done, 1)

            def pair(g, h, landed, first=False):
                if first:
                    up(g, h, landed, (0,))
                    gate(g, h, landed)
                    up(g, h, landed, (1,))
                else:
                    up(g, h, landed)
                    gate(g, h, landed)
                    add_before(g)
                gather(g + 2)
                turn_hidden(g)

            gather(1)
            pe.wait_ge(more_ready, 1)
            more = pe.value_load(more_i[0:1, 0:1], min_val=0, max_val=MAX_PASS - 1)
            pair(0, 0, 16, first=True)
            down(0)
            with pe.Fori(0, more * (PAIRS // 2) + PAIRS // 2 - 2) as i:
                for h in (1, 0):
                    g = i * 2 + (1 if h else 2)
                    pair(g, h, i * 16 + (16 if h else 32))
                    down(g)
            g = more * PAIRS + PAIRS - 3
            pair(g, 1, more * (PAIRS * 8) + (PAIRS * 8 - 16))
            down(g)
            landed = more * (PAIRS * 8) + PAIRS * 8
            g = more * PAIRS + PAIRS - 1
            pair(g - 1, 0, landed)
            gate(g, 1, landed)
            down(g - 1)
            add_before(g)
            up(g, 1, landed)
            turn_hidden(g)
            pe.wait_ge(hidT_ready, g + 2)
            for n in range(2):
                for k in range(2):
                    pe.wait_ge(last_full[n][k], 16)
                expert_out(n, last_w).then_inc(down_done, 1)
            pe.wait_ge(placeT_ready, g + 2)
            for n in range(2):
                pe.wait_ge(y_ready, g + 1 + n)
                for t in range(TT):
                    scatter(t, n, True).then_inc(acc_done, 1)

        @block.scalar
        def _(act):
            steps = [0]

            def step(ins):
                ins.then_inc(act_step, 1)
                steps[0] += 1
                act.wait_ge(act_step, steps[0])

            act.wait_ge(c_in, 16)
            nc.scalar.activation(cvec[:, 1, :], cvec[:, 0, :], ACT.Exp, scale=-1.0).then_inc(c_exp, 1)

            def root(which, t, part):
                nc.scalar.activation(rms[:, which, t:t + 1], mean_sq[:, which, t, part:part + 1], ACT.Sqrt,
                                     bias=eps_col[:, 0:1] if part == 0 else mean_sq[:, which, t, 2:3]
                                     ).then_inc(root_ready, 1)

            n_sq = [0]

            def square(which, t, part, cols):
                src = acc[:, t, cols] if which == 2 else x_sb[:, t, cols]
                nc.scalar.activation(xn[:, t, cols], src, ACT.Square, scale=D ** -0.5,
                                     accum_out=mean_sq[:, which, t, part:part + 1]).then_inc(squares, 1)
                n_sq[0] += 1

            def half_norm(which, t, n):
                square(which, t, n, slice(n * U, (n + 1) * U))
                act.wait_ge(squares, n_sq[0])
                if n == 0:
                    nc.scalar.activation(mean_sq[:, which, t, 2:3], mean_sq[:, which, t, 0:1], ACT.Identity,
                                         bias=eps_col[:, 0:1]).then_inc(squares, 1)
                    n_sq[0] += 1
                else:
                    root(which, t, 1)

            act.wait_ge(x_in, 16)
            for t in range(TT):
                square(0, t, 0, slice(0, D))
            act.wait_ge(squares, n_sq[0])
            act.wait_ge(consts, 1)
            for t in range(TT):
                root(0, t, 0)

            def part_copy(u, src=ps_part):
                act.wait_ge(*unit_used(unit_index[("ada", u)]))
                if u >= 2:
                    act.wait_ge(fold_done, u - 1)
                nc.scalar.copy(part[:, u % 2, :], src).then_inc(part_read, 1)

            def hT_by_act(which, src):
                for j in (0, 1, 4, 5):
                    if which == 0:
                        nc.scalar.activation(hT[:, j, :], src[:, j * S:(j + 1) * S], ACT.Identity,
                                             scale=scale_a[:, 0, j:j + 1], bias=modcol[:, 0, j:j + 1]).then_inc(hT_act, 1)
                    else:
                        nc.scalar.activation(hT[:, j, :], src[:, j * S:(j + 1) * S], ACT.Copy,
                                             scale=scale_a[:, 1, j:j + 1]).then_inc(hT_act, 1)

            def channels(ap):
                return ap.rearrange("p (m s) -> p m s", m=CT4)

            def tokens(ap):
                return ap.rearrange("p (t n) -> p t n", t=TT)

            for u in range(4):
                part_copy(u, partials(u))
            act.wait_ge(xT_done, 1)
            act.wait_ge(scales_ready, 1)
            hT_by_act(0, banks(2, 4))
            act.wait_ge(trig_arg_ready, 1)
            nc.scalar.activation(trig, trig_arg[:, 3], ACT.Sin).then_inc(trig_ready, 1)
            act.wait_ge(decay_ready, 1)
            for h in range(H):
                lg_h = float(np.log1p(-np.exp2(np.float32(-5.0 - h))).astype(np.float32))
                nc.scalar.activation(decay[:, h, :], dist, ACT.Exp, scale=lg_h).then_inc(decay_masked, 1)
            act.wait_ge(win_done, win_turn["h"])
            nc.scalar.copy(conv_y[:, :, :], channels(ps_p)).then_inc(h_read, 1)
            act.wait_ge(qT_done, 1)
            nc.scalar.copy(qT[:, :, :], channels(ps_s)).then_inc(qT_ready, 1)
            act.wait_ge(kT_done, 1)
            nc.scalar.copy(kT, channels(ps_s)).then_inc(kT_ready, 1)
            act.wait_ge(win_done, win_turn["b"])
            nc.scalar.copy(b_sb, channels(ps_p)).then_inc(b_ready, 1)
            act.wait_ge(convy_ready, 1)
            nc.scalar.activation(b_sb, conv_y[:, :, :], ACT.Square).then_inc(convsq_ready, 1)
            act.wait_ge(win_done, win_turn["g"])
            nc.scalar.activation(g_silu, tokens(ps_q), ACT.Exp, scale=-1.0).then_inc(g_exp, 1)
            nc.scalar.copy(g_raw, tokens(ps_q)).then_inc(g_read, 1)
            act.wait_ge(v_first, 1)
            nc.scalar.copy(v_sb[:, 0], ps_p[:, 0:RW]).then_inc(v_ready, 1)
            act.wait_ge(convms_done, 1)
            nc.scalar.activation(b_sb, channels(ps_s), ACT.Sqrt, bias=eps_col[:, 0:1]).then_inc(convroot_ready, 1)
            act.wait_ge(win_done, win_turn["v"])
            nc.scalar.copy(v_sb[:, 1], ps_p[:, RW:2 * RW]).then_inc(v_ready, 1)
            act.wait_ge(centered, 1)
            nc.scalar.activation(k_rot, q_rot, ACT.Square).then_inc(centered_sq, 1)
            act.wait_ge(gnvar_ready, 1)
            nc.scalar.activation(groups[:, 2, :], groups[:, 1, :], ACT.Sqrt, bias=eps_col[:, 1:2],
                                 scale=1.0 / DH).then_inc(gnroot_ready, 1)
            act.wait_ge(yretT_done, 1)
            for m in range(CT4):
                nc.scalar.activation(yT(m), ps_yT[:, m * S:(m + 1) * S], ACT.Copy,
                                     scale=small_cols[:, m:m + 1]).then_inc(yT_ret, 1)
            for n in range(2):
                for t in range(TT):
                    act.wait_ge(x1_ready, TT * n + t + 1)
                    half_norm(1, t, n)
            act.wait_ge(shift_done, 1)
            act.wait_ge(router_in, 16 * 4)
            nc.scalar.activation(shift_col[:, :], ps_s[0:G + E, U:U + 1], ACT.Identity,
                                 bias=router_b[:, 0:1]).then_inc(shift_read, 1)
            act.wait_ge(xT_done, 2)
            hT_by_act(1, banks(0, 4))
            act.wait_ge(fold_done, 11)
            nc.scalar.copy(gate_fold[:, 0:U], ps_s[:, 0:U]).then_inc(fold_read, 1)
            act.wait_ge(logitsT_done, 1)
            nc.scalar.copy(lgT[:, :], ps_q[0:G + E, 0:S]).then_inc(logitsT_ready, 1)
            act.wait_ge(group_shift, 1)
            nc.scalar.activation(rt[:, 1, :, 0:G], rt[:, 0, :, 0:G], ACT.Exp).then_inc(group_exp, 1)
            act.wait_ge(expert_shift, 1)
            nc.scalar.activation(rt[:, 5, :, :], rt[:, 4, :, :], ACT.Exp).then_inc(expert_exp, 1)
            act.wait_ge(fold_done, 12)
            nc.scalar.copy(gate_fold[:, U:D], ps_s[:, U:2 * U]).then_inc(fold_read, 1)

            def gathered_lo(g1):
                act.wait_ge(gather_done, g1 * 2 - 1)
                for j in range(KD // 2):
                    last = nc.scalar.activation(xgT[:, j, :], ps_xy[:, j * P:(j + 1) * P], ACT.Identity,
                                                scale=scale_a[:, 1, j:j + 1], bias=modcol[:, 2, j:j + 1])
                last.then_inc(xg_lo, 1)

            def pair(g, last_pair=False):
                act.wait_ge(gate_done, g + 1)
                nc.scalar.activation(ea, ps_gate, ACT.Exp, scale=-1.0).then_inc(ea_ready, 1)
                if last_pair:
                    nc.scalar.activation(rms[:, 0, 0:1], eps_col[:, 0:1], ACT.Sqrt)
                if not last_pair:
                    gathered_lo(g + 2)
                act.wait_ge(turned, g + 1)
                nc.scalar.copy(placeT, ps_up[:, 0:TT * P]).then_inc(placeT_ready, 1)

            gathered_lo(1)
            act.wait_ge(more_ready, 1)
            more = act.value_load(more_i[0:1, 0:1], min_val=0, max_val=MAX_PASS - 1)
            with act.Fori(0, more * (PAIRS // 2) + PAIRS // 2 - 1) as i:
                for h in range(2):
                    pair(i * 2 + h)
            pair(more * PAIRS + PAIRS - 2)
            pair(more * PAIRS + PAIRS - 1, last_pair=True)
            for n in range(2):
                for t in range(TT):
                    act.wait_ge(acc_done, n * TT + t + 1)
                    half_norm(2, t, n)

        @block.vector
        def _(dve):
            v = nc.vector
            steps = [0]

            def step(ins):
                ins.then_inc(dve_step, 1)
                steps[0] += 1
                dve.wait_ge(dve_step, steps[0])

            tt, ts, stt = v.tensor_tensor, v.tensor_scalar, v.scalar_tensor_tensor

            dve.wait_ge(c_exp, 1)
            step(ts(cvec[:, 2, :], cvec[:, 1, :], 1.0, None, ALU.add))
            step(v.reciprocal(cvec[:, 3, :], cvec[:, 2, :]))
            step(tt(cvec[:, 2, :], cvec[:, 3, :], cvec[:, 0, :], ALU.mult))
            v.tensor_copy(c_wide, cvec[:, 2, :].unsqueeze(2).broadcast_to([P, KD, 32])).then_inc(c_ready, 1)

            def norm_rows(which, t, count):
                dve.wait_ge(root_ready, count)
                step(v.reciprocal(inv_rms[:, which, t:t + 1], rms[:, which, t:t + 1]))
                ts(xn[:, t, :], x_sb[:, t, :], inv_rms[:, which, t:t + 1], None, ALU.mult).then_inc(xn_ready, 1)

            for t in range(TT):
                norm_rows(0, t, TT)
            dve.wait_ge(consts, 1)

            def fold_read_out(u):
                vec, half = u // 2, u % 2
                dve.wait_ge(fold_done, u + 1)
                if vec in (2, 5):
                    dst = (gate_mix if vec == 2 else gate_ffn)[:, half * U:(half + 1) * U]
                    tt(dst, ps_fold, dst, ALU.add).then_inc(fold_read, 1)
                else:
                    lo = 64 * half
                    tt(modcol[lo:lo + 64, {0: 0, 1: 1, 3: 2, 4: 3}[vec], :], ps_fold[lo:lo + 64, 0:KD],
                       mod_bias[lo:lo + 64, vec, :], ALU.add).then_inc(fold_read, 1)

            def ada_sums(u):
                n = unit_index[("ada", u)]
                w = ring[n % RING][:, :].rearrange("p (j f) -> p j f", j=KD)
                dst = part[:, u % 2, :]
                dve.wait_ge(ring_full[n % RING], 16 * (n // RING + 1))
                dve.wait_ge(fold_done, u - 1)
                step(ts(dst, w[:, 0, :], cvec[:, 2, 0:1], None, ALU.mult))
                for j in range(1, KD - 1):
                    step(stt(dst, w[:, j, :], cvec[:, 2, j:j + 1], dst, ALU.mult, ALU.add))
                stt(dst, w[:, KD - 1, :], cvec[:, 2, KD - 1:KD], dst, ALU.mult, ALU.add).then_inc(part_read, 1)

            def scales(which, count):
                dve.wait_ge(fold_read, count)
                stt(scale_a[:, which, :], modcol[:, 2 * which + 1, :], 1.0, norm_g[:, which, :],
                    ALU.add, ALU.mult).then_inc(scales_ready, 1)

            def hT_by_dve(which, src):
                for j in (2, 3, 6, 7):
                    if which == 0:
                        ts(hT[:, j, :], src[:, j * S:(j + 1) * S], scale_a[:, 0, j:j + 1],
                           modcol[:, 0, j:j + 1], ALU.mult, ALU.add).then_inc(hT_dve, 1)
                    else:
                        ts(hT[:, j, :], src[:, j * S:(j + 1) * S], scale_a[:, 1, j:j + 1], None,
                           ALU.mult).then_inc(hT_dve, 1)

            dve.wait_ge(mod_in, 16 * 3)
            for u in range(4):
                fold_read_out(u)
            scales(0, 4)
            dve.wait_ge(scales_ready, 1)
            dve.wait_ge(xT_done, 1)
            hT_by_dve(0, banks(2, 4))
            dve.wait_ge(pos_in, 16)
            step(v.tensor_copy(pos_f, pos_i[:, :]))
            angle, turns, red, arg = (trig_arg[:, i] for i in range(4))
            for t in range(TT):
                ts(angle[:, 1, t, :], inv_freq, pos_f[:, t:t + 1], None, ALU.mult).then_inc(dve_step, 1)
                steps[0] += 1
            dve.wait_ge(dve_step, steps[0])
            for i, quarter in ((0, 0.25), (1, 0.0)):
                step(ts(turns[:, i], angle[:, 1], 1.0 / TWO_PI, quarter, ALU.mult, ALU.add))
                step(ts(red[:, i], turns[:, i], ROUND, None, ALU.add))
                step(ts(turns[:, i], red[:, i], -ROUND, None, ALU.add))
                step(stt(red[:, i], turns[:, i], -TWO_PI_HI, angle[:, 1], ALU.mult, ALU.add))
                step(stt(arg[:, i], turns[:, i], -TWO_PI_MID, red[:, i], ALU.mult, ALU.add))
                step(stt(red[:, i], turns[:, i], -TWO_PI_LO, arg[:, i], ALU.mult, ALU.add))
                step(ts(turns[:, i], red[:, i], (1 - i) * np.pi / 2, -PI_BELOW, ALU.add, ALU.max))
                last = ts(arg[:, i], turns[:, i], PI_BELOW, None, ALU.min)
                if i == 0:
                    step(last)
            last.then_inc(trig_arg_ready, 1)
            stt(dist, dist, -1.0, dist, ALU.mult, ALU.max).then_inc(decay_ready, 1)
            dve.wait_ge(trig_ready, 1)

            def rotate(src, dst, ready):
                for t in range(TT):
                    s3 = src[:, t * RW:(t + 1) * RW].rearrange("p (a f) -> p a f", f=HALF)
                    cos = trig[:, 0, t, :].unsqueeze(1).broadcast_to([P, 2 * H, HALF])
                    sin = trig[:, 1, t, :].unsqueeze(1).broadcast_to([P, 2 * H, HALF])
                    if t:
                        dve.wait_ge(ready, 2 * t)
                    tt(tmp_c.rearrange("p (a f) -> p a f", f=HALF), s3, cos, ALU.mult).then_inc(dve_step, 1)
                    step_n()
                    step(tt(tmp_s.rearrange("p (a f) -> p a f", f=HALF), s3, sin, ALU.mult))
                    c4 = tmp_c.rearrange("p (h a f) -> p h a f", a=2, f=HALF)
                    s4 = tmp_s.rearrange("p (h a f) -> p h a f", a=2, f=HALF)
                    d4 = dst[:, t].rearrange("p (h a f) -> p h a f", a=2, f=HALF)
                    tt(d4[:, :, 0, :], c4[:, :, 0, :], s4[:, :, 1, :], ALU.subtract).then_inc(ready, 1)
                    tt(d4[:, :, 1, :], c4[:, :, 1, :], s4[:, :, 0, :], ALU.add).then_inc(ready, 1)

            def step_n():
                steps[0] += 1

            def weigh(h):
                dve.wait_ge(scores_done, h + 1)
                src = ps_s[:, (h % 2) * 512:(h % 2) * 512 + S + P]
                stt(weighted[h][:, 0:S], src[:, 0:S], DH ** -0.5, decay[:, h, :],
                    ALU.mult, ALU.mult).then_inc(dve_step, 1)
                step_n()
                stt(weighted[h][:, S:S + P], src[:, S:S + P], DH ** -0.5, decay[:, h, 0:P],
                    ALU.mult, ALU.mult).then_inc(weighted_ready, 1)

            taps = small_cols[:, 3 * CT4:(3 + KC) * CT4].rearrange("p (k m) -> p k m", k=KC)

            def conv(m):
                step(ts(conv_y[:, m, :], u_pad[:, m, KC - 1:KC - 1 + S], taps[:, KC - 1, m:m + 1],
                        small_cols[:, 2 * CT4 + m:2 * CT4 + m + 1], ALU.mult, ALU.add))
                for k in range(KC - 1):
                    step(stt(conv_y[:, m, :], u_pad[:, m, k:k + S], taps[:, k, m:m + 1], conv_y[:, m, :],
                             ALU.mult, ALU.add))

            dve.wait_ge(wide_ready, 3)
            dve.wait_ge(win_done, win_turn["q"])
            rotate(ps_p, q_rot, q_ready)
            dve.wait_ge(q_ready, 2 * TT)
            dve.wait_ge(smallT_done, 1)
            v.tensor_copy(small_cols[:, :], ps_s[:, 0:(KC + 3) * CT4]).then_inc(smallT_read, 1)
            ada_sums(4)
            dve.wait_ge(win_done, win_turn["k"])
            rotate(ps_q, k_rot, k_ready)
            fold_read_out(4)
            ada_sums(5)
            fold_read_out(5)
            dve.wait_ge(decay_masked, H)
            v.memset(decay[64:128, :, 0:64], 0.0).then_inc(dve_step, 1)
            steps[0] += 1
            dve.wait_ge(dve_step, steps[0])
            ada_sums(6)

            dve.wait_ge(smallT_read, 1)
            dve.wait_ge(h_read, 1)
            dve.wait_ge(win_done, win_turn["c"])
            tt(u_pad[:, :, KC - 1:KC - 1 + S], conv_y[:, :, :], ps_q.rearrange("p (m s) -> p m s", m=CT4),
               ALU.mult).then_inc(u_ready, 1)
            fold_read_out(6)
            dve.wait_ge(u_ready, 1)
            for m in range(CT4):
                conv(m)
            ada_sums(7)
            fold_read_out(7)
            weigh(0)
            weigh(1)
            dve.wait_ge(b_ready, 1)
            tt(conv_y[:, :, :], conv_y[:, :, :], b_sb, ALU.mult).then_inc(convy_ready, 1)
            ada_sums(8)
            weigh(2)
            weigh(3)
            ada_sums(9)
            weigh(4)
            weigh(5)
            fold_read_out(8)
            weigh(6)
            weigh(7)
            dve.wait_ge(g_exp, 1)
            step(ts(g_silu, g_silu, 1.0, None, ALU.add))
            step(v.reciprocal(g_silu, g_silu))
            dve.wait_ge(g_read, 1)
            tt(g_silu, g_silu, g_raw, ALU.mult).then_inc(g_ready, 1)
            dve.wait_ge(convroot_ready, 1)
            step(v.reciprocal(b_sb, b_sb))
            for m in range(CT4):
                last = stt(qT[:, m, :], conv_y[:, m, :], small_cols[:, CT4 + m:CT4 + m + 1], b_sb[:, m, :],
                           ALU.mult, ALU.mult)
            last.then_inc(yT_conv, 1)
            fold_read_out(9)

            dve.wait_ge(pv_done, H)
            y3 = ps_q.rearrange("p (a f) -> p a f", f=DH)
            q3 = q_rot.rearrange("p t (h f) -> p (t h) f", f=DH)
            k3 = k_rot.rearrange("p t (h f) -> p (t h) f", f=DH)
            g3 = g_silu.rearrange("p t (h f) -> p (t h) f", f=DH)

            def per_head(ap):
                return ap.unsqueeze(2).broadcast_to([P, TT * H, DH])

            step(v.tensor_reduce(groups[:, 0, :], y3, AX.X, ALU.add))
            step(ts(groups[:, 1, :], groups[:, 0, :], 1.0 / DH, None, ALU.mult))
            tt(q3, y3, per_head(groups[:, 1, :]), ALU.subtract).then_inc(centered, 1)
            dve.wait_ge(centered_sq, 1)
            v.tensor_reduce(groups[:, 1, :], k3, AX.X, ALU.add).then_inc(gnvar_ready, 1)
            dve.wait_ge(g_ready, 1)
            step(tt(g3, g3, q3, ALU.mult))
            dve.wait_ge(gnroot_ready, 1)
            step(v.reciprocal(groups[:, 0, :], groups[:, 2, :]))
            tt(q3, g3, per_head(groups[:, 0, :]), ALU.mult).then_inc(yret_ready, 1)
            scales(1, 10)
            dve.wait_ge(scales_ready, 2)
            ada_sums(10)
            ada_sums(11)

            def residual(t, n, src, gate):
                cols = slice(n * U, (n + 1) * U)
                step(tt(xn[:, t, cols], src, gate[:, cols], ALU.mult))
                tt(x_sb[:, t, cols], x_sb[:, t, cols], xn[:, t, cols], ALU.add).then_inc(x1_ready, 1)

            for n, src in ((0, ps_s), (1, ps_q)):
                for t in range(TT):
                    dve.wait_ge(wout_done, n * TT + t + 1)
                    residual(t, n, src[:, t * U:(t + 1) * U], gate_mix)
                    if n == 1 and t == 0:
                        norm_rows(1, 0, TT + 1)
            dve.wait_ge(shift_read, 1)
            ts(shift_diag[:, :], ident[0:G + E, 0:G + E], shift_col[:, 0:1], None, ALU.mult).then_inc(diag_ready, 1)
            dve.wait_ge(xT_done, 2)
            hT_by_dve(1, banks(0, 4))
            norm_rows(1, 1, TT + 2)
            dve.wait_ge(shift_spread, 1)
            v.tensor_copy(shift_rows[:, :], ps_q[:, U:U + G + E]).then_inc(shift_ready, 1)
            dve.wait_ge(shift_ready, 1)

            dve.wait_ge(logits_done, 1)

            def wide(ap, n):
                return ap.broadcast_to([P, TT, n])

            raw = ps_q[:, U:U + TT * (G + E)].rearrange("p (t n) -> p t n", t=TT)
            for t in range(TT):
                stt(lg_sb[:, t, :], raw[:, t, :], inv_rms[:, 1, t:t + 1], shift_rows[:, :],
                    ALU.mult, ALU.add).then_inc(dve_step, 1)
            steps[0] += TT
            dve.wait_ge(dve_step, steps[0])
            lg = lg_sb[:, :, :]
            glg, elg = lg[:, :, 0:G], lg[:, :, G:G + E].rearrange("p t (g e) -> p t g e", g=G)
            col = lambda i: rt[:, 15, :, i:i + 1]
            step(v.tensor_reduce(col(0), glg, AX.X, ALU.max))
            tt(rt[:, 0, :, 0:G], glg, wide(col(0), G), ALU.subtract).then_inc(group_shift, 1)
            dve.wait_ge(group_exp, 1)

            def first_max(probs, n, top, work, onehot):
                step(v.tensor_reduce(top, probs, AX.X, ALU.max))
                for t in range(TT):
                    stt(work[:, t], probs[:, t], top[:, t], rev[:, EG - n:EG],
                        ALU.is_equal, ALU.mult).then_inc(dve_step, 1)
                steps[0] += TT
                dve.wait_ge(dve_step, steps[0])
                step(v.tensor_reduce(col(7), work, AX.X, ALU.max))
                step(tt(onehot, work, wide(col(7), n), ALU.is_equal))

            gp = rt[:, 1, :, 0:G]
            group_hot = rt[:, 3, :, 0:G]
            first_max(gp, G, col(1), rt[:, 2, :, 0:G], group_hot)
            ohe4 = ohe.rearrange("p t (g e) -> p t g e", g=G)
            step(tt(ohe4, elg, group_hot.unsqueeze(3).broadcast_to([P, TT, G, EG]), ALU.mult))
            step(v.tensor_reduce(rt[:, 6, :, :], ohe.rearrange("p t (g e) -> p t e g", g=G), AX.X, ALU.add))
            step(v.tensor_reduce(col(0), rt[:, 6, :, :], AX.X, ALU.max))
            tt(rt[:, 4, :, :], rt[:, 6, :, :], wide(col(0), EG), ALU.subtract).then_inc(expert_shift, 1)
            dve.wait_ge(expert_exp, 1)
            first_max(rt[:, 5, :, :], EG, col(3), rt[:, 7, :, :], rt[:, 8, :, :])
            step(stt(rt[:, 9, :, :], rt[:, 8, :, :], -4.0, rt[:, 5, :, :], ALU.mult, ALU.add))
            first_max(rt[:, 9, :, :], EG, col(4), rt[:, 7, :, :], rt[:, 10, :, :])
            step(tt(within8[:, 1], rt[:, 8, :, :], rt[:, 10, :, :], ALU.add))
            gh4 = group_hot.unsqueeze(3).broadcast_to([P, TT, G, EG])

            def spread(i):
                return within8[:, i].unsqueeze(2).broadcast_to([P, TT, G, EG])

            tt(msk.rearrange("p t (g e) -> p t g e", g=G), spread(1), gh4, ALU.mult).then_inc(mask_ready, 1)
            dve.wait_ge(mask_ready, 1)
            dve.wait_ge(rank_done, 1)
            step(stt(posm[:, :, :], ps_s[:, 0:TT * E].rearrange("p (t e) -> p t e", t=TT), 1.0, msk[:, :, :],
                     ALU.add, ALU.mult))

            def pick_pair(e, ids):
                for k in range(2):
                    for t in range(TT):
                        last = ts(pick[:, t, k * SLOTS:(k + 1) * SLOTS], slot_ids[:, ids],
                                  posm[:, t, bass.ds(e + k, 1)], None, ALU.is_equal)
                last.then_inc(pick_ready, 1)

            def gathered_hi(g1):
                dve.wait_ge(gather_done, g1 * 2)
                for j in range(KD // 2, KD):
                    last = ts(xgT[:, j, :], ps_xy[:, j * P:(j + 1) * P], scale_a[:, 1, j:j + 1],
                              modcol[:, 2, j:j + 1], ALU.mult, ALU.add)
                last.then_inc(xg_hi, 1)

            pick_pair(0, slice(0, SLOTS))
            dve.wait_ge(count_done, 1)
            step(v.tensor_reduce(cnt[:, 0:1], ps_s[:, 512:512 + E], AX.X, ALU.max))
            step(ts(rt[0:1, 13, 0, 0:MAX_PASS - 1], slot_ids[0:1, SLOTS:MAX_PASS * SLOTS:SLOTS], cnt[0:1, 0:1], None,
                    ALU.is_le))
            step(v.tensor_reduce(cnt[0:1, 1:2], rt[0:1, 13, 0, 0:MAX_PASS - 1], AX.X, ALU.add))
            v.tensor_copy(more_i[0:1, 0:1], cnt[0:1, 1:2]).then_inc(more_ready, 1)
            step(v.tensor_reduce(col(2), gp, AX.X, ALU.add))
            step(tt(col(5), col(3), col(4), ALU.add))
            step(tt(col(6), col(5), col(2), ALU.mult))
            step(v.reciprocal(col(5), col(6)))
            step(tt(col(6), col(5), col(1), ALU.mult))
            step(tt(col(0), col(3), col(6), ALU.mult))
            step(tt(col(5), col(4), col(6), ALU.mult))
            step(tt(rt[:, 11, :, :], rt[:, 8, :, :], wide(col(0), EG), ALU.mult))
            step(tt(rt[:, 12, :, :], rt[:, 10, :, :], wide(col(5), EG), ALU.mult))
            step(tt(within8[:, 0], rt[:, 11, :, :], rt[:, 12, :, :], ALU.add))
            step(tt(combine[:, :, :].rearrange("p t (g e) -> p t g e", g=G), spread(0), gh4, ALU.mult))
            dve.sem_inc(hidT_ready, 1)
            dve.sem_inc(placeT_ready, 1)
            dve.wait_ge(more_ready, 1)
            more = dve.value_load(more_i[0:1, 0:1], min_val=0, max_val=MAX_PASS - 1)
            dve.wait_ge(gate_ready, 1)
            gathered_hi(1)
            base = steps[0]

            def pair(g, last_pair=False):
                if not last_pair:
                    pick_pair(((g + 1) % PAIRS) * 2, bass.ds(((g + 1) // PAIRS) * SLOTS, SLOTS))
                e = (g % PAIRS) * 2
                ids = bass.ds((g // PAIRS) * SLOTS, SLOTS)
                for k in range(2):
                    for t in range(TT):
                        last = ts(place[:, t, k * SLOTS:(k + 1) * SLOTS], slot_ids[:, ids],
                                  posm[:, t, bass.ds(e + k, 1)], combine[:, t, bass.ds(e + k, 1)],
                                  ALU.is_equal, ALU.mult)
                last.then_inc(place_ready, 1)
                dve.wait_ge(ea_ready, g + 1)
                ts(hid, ea, 1.0, None, ALU.add).then_inc(dve_step, 1)
                dve.wait_ge(dve_step, g * 3 + (base + 1))
                v.reciprocal(ea, hid).then_inc(dve_step, 1)
                dve.wait_ge(dve_step, g * 3 + (base + 2))
                tt(hid, ea, ps_gate, ALU.mult).then_inc(dve_step, 1)
                dve.wait_ge(dve_step, g * 3 + (base + 3))
                dve.wait_ge(up_done, g * 2 + 2)
                tt(hid, hid, ps_up, ALU.mult).then_inc(hid_ready, 1)
                if not last_pair:
                    gathered_hi(g + 2)
                dve.wait_ge(turned, g + 1)
                v.tensor_copy(hidT, ps_gate.rearrange("p (j s) -> p j s", j=KF)).then_inc(hidT_ready, 1)
                for n, cols in enumerate((slice(0, U), slice(U, D)) if last_pair else (slice(0, D),)):
                    dve.wait_ge(down_done, g + n + 1)
                    tt(y_sb[:, cols], ps_xy[:, cols], gate_ffn[:, cols], ALU.mult).then_inc(y_ready, 1)

            with dve.Fori(0, more * (PAIRS // 2) + PAIRS // 2 - 1) as i:
                for h in range(2):
                    pair(i * 2 + h)
            pair(more * PAIRS + PAIRS - 2)
            pair(more * PAIRS + PAIRS - 1, last_pair=True)

            for t in range(TT):
                dve.wait_ge(root_ready, 2 * TT + t + 1)
                v.reciprocal(inv_rms[:, 2, t:t + 1], rms[:, 2, t:t + 1]).then_inc(last_step, 1)
                dve.wait_ge(last_step, t + 1)
                stt(xn[:, t, :], acc[:, t, :], inv_rms[:, 2, t:t + 1], final_g[:, :],
                    ALU.mult, ALU.mult).then_inc(out_ready, 1)


_INS = ["x", "c", "positions", "ada_w", "ada_b", "norm_mix_g", "norm_ffn_g", "w_in", "conv_w", "conv_b", "beta_ret",
        "beta_conv", "w_out", "router_group_w", "router_group_b", "router_expert_w", "router_expert_b",
        "expert_w_gate", "expert_w_up", "expert_w_down", "norm_final_g"]


def kernel(**inputs):
    import numpy as _np
    import concourse.bacc as _bacc
    from concourse import mybir as _mybir
    from concourse.bass_utils import run_bass_kernel_spmd as _run

    nc = _bacc.Bacc("TRN2", target_bir_lowering=False, num_devices=1)
    arrays, args = {}, []
    for name in _INS:
        a = _np.ascontiguousarray(inputs[name])
        arrays[f"in_{name}"] = a
        args.append(nc.dram_tensor(f"in_{name}", a.shape, _mybir.dt.from_np(a.dtype), kind="ExternalInput").ap())
    out = nc.dram_tensor("out_0", inputs["x"].shape, F32, kind="ExternalOutput").ap()
    hybrid_retention_moe_layer(nc, *args, out)
    r = _run(nc, [arrays], core_ids=[0])
    return r.results[0]["out_0"]
```
